# Optimizing a Trainium2 kernel written in Bass

```python
import math
import jax, jax.numpy as jnp
from jax import lax
import numpy as np

D_MODEL = 1024
BATCH = 1
SEQ = 512
DEPTH = 1

HEAD_DIM = 64
MOBA_HEADS = D_MODEL // (2 * HEAD_DIM)
DIFF_HEADS = D_MODEL // (4 * HEAD_DIM)
MOBA_WIDTH = MOBA_HEADS * HEAD_DIM
DIFF_QK_WIDTH = DIFF_HEADS * 2 * HEAD_DIM
DIFF_V_DIM = 2 * HEAD_DIM
DIFF_WIDTH = DIFF_HEADS * DIFF_V_DIM
MIX_WIDTH = MOBA_WIDTH + DIFF_WIDTH
IN_PROJ_WIDTH = 3 * MOBA_WIDTH + 2 * DIFF_QK_WIDTH + DIFF_WIDTH
MOBA_BLOCK = 256
MOBA_TOPK = 3
MOBA_QCHUNK = 32
DENSE_QBLOCK = 128
FFN_HIDDEN = ((8 * D_MODEL + 3 * 256 - 1) // (3 * 256)) * 256
ROPE_THETA = 10000.0
RMS_EPS = 1e-6

kernel_name = "hymba_moba_diffattn_swiglu"

def rms_norm(x, gain):
    xf = x.astype(jnp.float32)
    xf = xf * lax.rsqrt(jnp.mean(xf * xf, axis=-1, keepdims=True) + RMS_EPS)
    return (xf * gain.astype(jnp.float32)).astype(x.dtype)

def rope_tables(seq, dim):
    inv = 1.0 / (ROPE_THETA ** (jnp.arange(0, dim, 2, dtype=jnp.float32) / dim))
    ang = jnp.arange(seq, dtype=jnp.float32)[:, None] * inv[None, :]
    ang = jnp.concatenate([ang, ang], axis=-1)
    return jnp.cos(ang), jnp.sin(ang)

def apply_rope(x, cos, sin):
    half = x.shape[-1] // 2
    rot = jnp.concatenate([-x[..., half:], x[..., :half]], axis=-1)
    return (x.astype(jnp.float32) * cos + rot.astype(jnp.float32) * sin).astype(x.dtype)

def moba_attention(q, k, v):
    B, H, S, D = q.shape
    s_pad = -(-S // MOBA_BLOCK) * MOBA_BLOCK
    pad = ((0, 0), (0, 0), (0, s_pad - S), (0, 0))
    q, k, v = jnp.pad(q, pad), jnp.pad(k, pad), jnp.pad(v, pad)
    nb = s_pad // MOBA_BLOCK
    top_k = min(MOBA_TOPK, nb)
    scale = D ** -0.5
    kb = k.reshape(B, H, nb, MOBA_BLOCK, D)
    vb = v.reshape(B, H, nb, MOBA_BLOCK, D)
    k_mean = jnp.mean(kb.astype(jnp.float32), axis=3).astype(k.dtype)
    b_ix = jnp.arange(B)[:, None, None, None]
    h_ix = jnp.arange(H)[None, :, None, None]
    C = MOBA_QCHUNK

    def chunk(c):
        start = c * C
        blk = start // MOBA_BLOCK
        qc = lax.dynamic_slice_in_dim(q, start, C, axis=2)
        gate = jnp.einsum('bhqd,bhnd->bhqn', qc, k_mean).astype(jnp.float32)
        gate = jnp.where(jnp.arange(nb) < blk, gate, -jnp.inf)
        _, sel = lax.top_k(gate, top_k)
        sel_valid = jnp.arange(top_k) < blk
        k_sel = kb[b_ix, h_ix, sel]
        v_sel = vb[b_ix, h_ix, sel]
        s_sel = jnp.einsum('bhqd,bhqrkd->bhqrk', qc, k_sel).astype(jnp.float32) * scale
        s_sel = jnp.where(sel_valid[:, None], s_sel, -jnp.inf)
        s_sel = s_sel.reshape(B, H, C, top_k * MOBA_BLOCK)
        k_own = lax.dynamic_index_in_dim(kb, blk, axis=2, keepdims=False)
        v_own = lax.dynamic_index_in_dim(vb, blk, axis=2, keepdims=False)
        s_own = jnp.einsum('bhqd,bhkd->bhqk', qc, k_own).astype(jnp.float32) * scale
        q_pos = start + jnp.arange(C)
        k_pos = blk * MOBA_BLOCK + jnp.arange(MOBA_BLOCK)
        s_own = jnp.where(k_pos[None, :] <= q_pos[:, None], s_own, -jnp.inf)
        p = jax.nn.softmax(jnp.concatenate([s_sel, s_own], axis=-1), axis=-1)
        p_sel = p[..., :top_k * MOBA_BLOCK].reshape(B, H, C, top_k, MOBA_BLOCK).astype(v.dtype)
        p_own = p[..., top_k * MOBA_BLOCK:].astype(v.dtype)
        return (jnp.einsum('bhqrk,bhqrkd->bhqd', p_sel, v_sel)
                + jnp.einsum('bhqk,bhkd->bhqd', p_own, v_own))

    outs = lax.map(chunk, jnp.arange(s_pad // C))
    out = outs.transpose(1, 2, 0, 3, 4).reshape(B, H, s_pad, D)
    return out[:, :, :S]

def diff_attention(q, k, v, lam):
    B, H, _, S, D = q.shape
    scale = D ** -0.5
    QB = DENSE_QBLOCK
    k_pos = jnp.arange(S)

    def qblock(i):
        start = i * QB
        qb = lax.dynamic_slice_in_dim(q, start, QB, axis=3)
        s = jnp.einsum('bhmqd,bhmkd->bhmqk', qb, k).astype(jnp.float32) * scale
        mask = k_pos[None, :] <= (start + jnp.arange(QB))[:, None]
        p = jax.nn.softmax(jnp.where(mask, s, -jnp.inf), axis=-1)
        a = p[:, :, 0] - lam * p[:, :, 1]
        return jnp.einsum('bhqk,bhkd->bhqd', a.astype(v.dtype), v)

    outs = lax.map(qblock, jnp.arange(S // QB))
    return outs.transpose(1, 2, 0, 3, 4).reshape(B, H, S, v.shape[-1])

def setup_inputs(seed: int = 0) -> dict:
    key = jax.random.key(seed)
    ks = jax.random.split(key, 17)
    f32 = jnp.float32

    def nrm(k, shape, scale):
        return jax.random.normal(k, shape, f32) * scale

    def gain(k, shape):
        return 1.0 + 0.02 * jax.random.normal(k, shape, f32)

    L = DEPTH
    return {
        "x": jax.random.normal(ks[0], (BATCH, SEQ, D_MODEL), f32),
        "attn_norm": gain(ks[1], (L, D_MODEL)),
        "w_in": nrm(ks[2], (L, D_MODEL, IN_PROJ_WIDTH), D_MODEL ** -0.5),
        "moba_q_norm": gain(ks[3], (L, HEAD_DIM)),
        "moba_k_norm": gain(ks[4], (L, HEAD_DIM)),
        "diff_q_norm": gain(ks[5], (L, HEAD_DIM)),
        "diff_k_norm": gain(ks[6], (L, HEAD_DIM)),
        "lambda_q1": nrm(ks[7], (L, HEAD_DIM), 0.1),
        "lambda_k1": nrm(ks[8], (L, HEAD_DIM), 0.1),
        "lambda_q2": nrm(ks[9], (L, HEAD_DIM), 0.1),
        "lambda_k2": nrm(ks[10], (L, HEAD_DIM), 0.1),
        "diff_subln": gain(ks[11], (L, DIFF_V_DIM)),
        "w_out": nrm(ks[12], (L, MIX_WIDTH, D_MODEL), MIX_WIDTH ** -0.5),
        "ffn_norm": gain(ks[13], (L, D_MODEL)),
        "w_gate": nrm(ks[14], (L, D_MODEL, FFN_HIDDEN), D_MODEL ** -0.5),
        "w_up": nrm(ks[15], (L, D_MODEL, FFN_HIDDEN), D_MODEL ** -0.5),
        "w_down": nrm(ks[16], (L, FFN_HIDDEN, D_MODEL), FFN_HIDDEN ** -0.5),
    }

def reference(x, attn_norm, w_in, moba_q_norm, moba_k_norm, diff_q_norm, diff_k_norm,
              lambda_q1, lambda_k1, lambda_q2, lambda_k2, diff_subln, w_out,
              ffn_norm, w_gate, w_up, w_down):
    B, S, _ = x.shape
    cos, sin = rope_tables(S, HEAD_DIM)
    splits = [MOBA_WIDTH, 2 * MOBA_WIDTH, 3 * MOBA_WIDTH,
              3 * MOBA_WIDTH + DIFF_QK_WIDTH, 3 * MOBA_WIDTH + 2 * DIFF_QK_WIDTH]
    for l in range(DEPTH):
        lambda_init = 0.8 - 0.6 * math.exp(-0.3 * l)
        h = rms_norm(x, attn_norm[l])
        proj = jnp.einsum('bsd,de->bse', h, w_in[l])
        mq, mk, mv, dq, dk, dv = jnp.split(proj, splits, axis=-1)

        mq = rms_norm(mq.reshape(B, S, MOBA_HEADS, HEAD_DIM), moba_q_norm[l]).transpose(0, 2, 1, 3)
        mk = rms_norm(mk.reshape(B, S, MOBA_HEADS, HEAD_DIM), moba_k_norm[l]).transpose(0, 2, 1, 3)
        mv = mv.reshape(B, S, MOBA_HEADS, HEAD_DIM).transpose(0, 2, 1, 3)
        mq, mk = apply_rope(mq, cos, sin), apply_rope(mk, cos, sin)
        moba_out = moba_attention(mq, mk, mv)
        moba_out = moba_out.transpose(0, 2, 1, 3).reshape(B, S, MOBA_WIDTH)

        dq = rms_norm(dq.reshape(B, S, DIFF_HEADS, 2, HEAD_DIM), diff_q_norm[l]).transpose(0, 2, 3, 1, 4)
        dk = rms_norm(dk.reshape(B, S, DIFF_HEADS, 2, HEAD_DIM), diff_k_norm[l]).transpose(0, 2, 3, 1, 4)
        dv = dv.reshape(B, S, DIFF_HEADS, DIFF_V_DIM).transpose(0, 2, 1, 3)
        dq, dk = apply_rope(dq, cos, sin), apply_rope(dk, cos, sin)
        lam = (jnp.exp(jnp.sum(lambda_q1[l].astype(jnp.float32) * lambda_k1[l].astype(jnp.float32)))
               - jnp.exp(jnp.sum(lambda_q2[l].astype(jnp.float32) * lambda_k2[l].astype(jnp.float32)))
               + lambda_init)
        diff_out = diff_attention(dq, dk, dv, lam)
        diff_out = rms_norm(diff_out, diff_subln[l]) * (1.0 - lambda_init)
        diff_out = diff_out.transpose(0, 2, 1, 3).reshape(B, S, DIFF_WIDTH)

        mixed = jnp.concatenate([moba_out, diff_out], axis=-1)
        x = x + jnp.einsum('bse,ed->bsd', mixed, w_out[l])

        h = rms_norm(x, ffn_norm[l])
        g = jnp.einsum('bsd,df->bsf', h, w_gate[l])
        u = jnp.einsum('bsd,df->bsf', h, w_up[l])
        x = x + jnp.einsum('bsf,fd->bsd', jax.nn.silu(g) * u, w_down[l])
    return x


_drawn_inputs = setup_inputs


def setup_inputs(seed=0):
    import zlib

    import numpy as np

    out = dict(_drawn_inputs(seed))
    spreads = {}
    factors = {'attn_norm': 2.757,
     'moba_q_norm': 8.0,
     'moba_k_norm': 8.0,
     'diff_q_norm': 4.857,
     'diff_k_norm': 4.754,
     'lambda_k1': 2.926,
     'lambda_q2': 7.528,
     'lambda_k2': 8.0,
     'diff_subln': 4.741,
     'ffn_norm': 4.152}
    for name, (base, spread) in spreads.items():
        noise = np.random.default_rng([zlib.crc32(name.encode()), seed]).standard_normal(out[name].shape)
        drawn = base * np.exp(spread * noise) if base else spread * noise
        out[name] = __import__('jax').numpy.asarray(drawn.astype(out[name].dtype))
    for name, factor in factors.items():
        out[name] = (out[name] * factor).astype(out[name].dtype)
    return out
```

```python
from contextlib import ExitStack

import concourse.bass as bass
from concourse import mybir

ALU = mybir.AluOpType
ACT = mybir.ActivationFunctionType
AX = mybir.AxisListType
F32 = mybir.dt.float32
F32R = mybir.dt.float32r
U32 = mybir.dt.uint32

P = 128
SEQ = 512
D = 1024
FFN = 2816
HEAD = 64
EPS = 1e-6
BLOCK = 256
TT = SEQ // P
KT = D // P
PAIRS = 8
MOBA_PAIRS = 4
FT = FFN // P
LAMBDA_INIT = 0.8 - 0.6 * 1.0
NEWTON = 3
NEWTON_OPS = 3 + 3 * NEWTON
RSQRT_MAGIC = 0x5F3759DF
MASKED = -(2.0 ** 127)

G_OUT = 3 * PAIRS
G_FFN = G_OUT + KT
G_DOWN = G_FFN + 2 * FT
TILES = G_DOWN + FT

assert SEQ // BLOCK == 2, "MoBA is causal attention for two blocks only"


def raw_slot(g):
    return g % 3 if g < G_OUT + 3 else g % 4


def raw_loads(g):
    if g < G_OUT + 3:
        return g // 3 + 1
    return 1 + (g - 27) // 4 if g % 4 == 3 else 10 + (g - 28) // 4


def build(nc, x, wt, vec, gain2, lams, ident_in, mask_in, cos_in, sin_in, ind_in, out):
    with ExitStack() as ctx:
        cursor = [16512]

        def place(name, shape, dt, at=None):
            n = 4
            for s in shape[1:]:
                n *= s
            if at is None:
                at = cursor[0]
                cursor[0] += n
            return nc.alloc_sbuf_tensor_at(name, shape, dt, offset=at), at

        def sem(name):
            return ctx.enter_context(nc.semaphore(name))

        X, _ = place("residual", [P, TT, D], F32)
        HH, _ = place("h_hi", [P, KT, SEQ], F32R)
        HL, _ = place("h_lo", [P, KT, SEQ], F32R)
        RAW, _ = place("w_raw", [P, 4, D], F32)
        WH, at_wh = place("w_hi", [P, 4, D], F32R)
        WL, at_wl = place("w_lo", [P, 4, D], F32R)
        ident, _ = place("ident", [P, P], F32)
        identR, _ = place("ident_r", [P, P], F32R)
        maskR, _ = place("mask_r", [P, P], F32R)
        cosT, _ = place("cos", [P, SEQ], F32)
        sinT, _ = place("sin", [P, SEQ], F32)
        small, _ = place("small", [P, 192], F32)
        QG, at_tmp = place("q_gained", [P, SEQ], F32)
        QR, _ = place("q_rotated", [P, SEQ], F32)
        QS, _ = place("q_roped", [P, SEQ], F32)
        KG, _ = place("k_gained", [P, SEQ], F32)
        KR, _ = place("k_rotated", [P, SEQ], F32)
        KS, _ = place("k_roped", [P, SEQ], F32)
        VT, _ = place("v_by_dim", [P, SEQ], F32)
        SG, _ = place("silu_gate", [P, 2, SEQ], F32, at_tmp)
        AC, _ = place("gated", [P, 2, SEQ], F32, at_tmp + 4096)
        AH, r0 = place("hidden_hi", [P, FT, SEQ], F32R)
        AL, _ = place("hidden_lo", [P, FT, SEQ], F32R)
        KB = 1024
        MH, _ = place("mixed_hi", [P, KT, SEQ], F32R, r0)
        ML, _ = place("mixed_lo", [P, KT, SEQ], F32R, r0 + 16 * KB)
        PTH, _ = place("probsT_hi", [P, 2, TT, SEQ], F32R, r0 + 32 * KB)
        PTL, _ = place("probsT_lo", [P, 2, TT, SEQ], F32R, r0 + 48 * KB)
        HN, _ = place("h_normed", [P, TT, D], F32, r0 + 32 * KB)
        JUNK, _ = place("squares", [P, D], F32, r0 + 48 * KB)
        G2, _ = place("ffn_gain", [P, D], F32, r0 + 52 * KB)
        VH, _ = place("v_hi", [P, 2, TT, P], F32R, r0 + 64 * KB)
        VL, _ = place("v_lo", [P, 2, TT, P], F32R, r0 + 68 * KB)
        QH, _ = place("q_hi", [P, SEQ], F32R, r0 + 72 * KB)
        QL, _ = place("q_lo", [P, SEQ], F32R, r0 + 74 * KB)
        KH, _ = place("k_hi", [P, SEQ], F32R, r0 + 76 * KB)
        KL, _ = place("k_lo", [P, SEQ], F32R, r0 + 78 * KB)
        SQQ, _ = place("q_squared", [P, SEQ], F32, r0 + 80 * KB)
        SQK, _ = place("k_squared", [P, SEQ], F32, r0 + 82 * KB)
        KBC, _ = place("k_rstd_spread", [P, TT, 2, HEAD], F32, r0 + 84 * KB)
        ON, _ = place("o_normed", [P, TT, P], F32, r0 + 86 * KB)
        MASK0, _ = place("mask_in", [P, P], F32, r0 + 86 * KB)
        LAM0, _ = place("lambda_in", [P, 4 * HEAD], F32, r0 + 84 * KB)
        PR0, _ = place("probs_0", [P, 2, SEQ], F32, at_wh + 3 * 4 * D)
        PR1, _ = place("probs_1", [P, 2, SEQ], F32, at_wl + 3 * 4 * D)
        PR = (PR0, PR1)

        VEC = small[:, 0:16]
        IND = small[:, 16:18]
        NA = small[:, 32:48]
        NT = small[:, 48:64]
        NY = small[:, 64:80]
        NZ = small[:, 80:96]
        RQ = small[:, 96:104]
        SUM = small[:, 104:112]
        RS = small[:, 112:120]
        MX = small[:, 120:128]
        NB = small[:, 128:136]
        SS = small[:, 136:140]
        SO = small[:, 140:144]
        LP = small[:, 144:148]
        LAM = small[:, 148:149]
        SUBG = small[:, 149:150]
        NL = small[:, 152:156]
        S2 = small[:, 156:160]

        ps = ctx.enter_context(nc.psum_tensor("ps", [P, 8, SEQ], F32))

        x_in = [sem(f"x_in{t}") for t in range(TT)]
        ident_in_s = sem("ident_in")
        small_in = sem("small_in")
        rope_in = sem("rope_in")
        misc_in = sem("misc_in")
        gain2_in = sem("gain2_in")
        raw_in = [sem(f"raw_in{s}") for s in range(4)]
        w_hi = sem("w_hi_ready")
        w_lo = sem("w_lo_ready")
        w_used = sem("w_used")
        x_sq = sem("x_squared")
        newton = sem("newton_step")
        hn = sem("h_normed_ready")
        x_turned = sem("x_turned")
        hh = sem("h_hi_ready")
        hl = sem("h_lo_ready")
        consts = sem("consts_ready")
        lam_dot = sem("lambda_dots")
        lam_exp = sem("lambda_exps")
        lam_s = sem("lambda_ready")
        pads = sem("v_pads_cleared")
        q_ev = sem("q_evacuated")
        k_ev = sem("k_evacuated")
        v_ev = sem("v_evacuated")
        q_rot = sem("q_rotated_in")
        k_rot = sem("k_rotated_in")
        q_pool = sem("q_rope_step")
        k_pool = sem("k_rope_step")
        qh_s, ql_s, kh_s, kl_s = sem("q_hi_ready"), sem("q_lo_ready"), sem("k_hi_ready"), sem("k_lo_ready")
        kn_s = sem("k_normed")
        ms_s = sem("mean_squares")
        rq_s = sem("q_scale_ready")
        kbc_s = sem("k_rstd_spread_ready")
        kb_s = sem("k_rstd_turned")
        v_turn = sem("v_turned")
        vh_s, vl_s = sem("v_hi_ready"), sem("v_lo_ready")
        sc_s = sem("scores_ready")
        mx_s = sem("max_found")
        nb_s = sem("bias_ready")
        ex_s = sem("exp_ready")
        rs_s = sem("sums_inverted")
        lr_s = sem("map1_scaled")
        pn_s = sem("probs_normed")
        pt_s = sem("probs_turned")
        ph_s, pl_s = sem("probsT_hi_ready"), sem("probsT_lo_ready")
        pv_s = sem("heads_out")
        o_sq = sem("o_squared")
        on_s = sem("o_normed_ready")
        o_turn = sem("o_turned")
        mh_s, ml_s = sem("mixed_hi_ready"), sem("mixed_lo_ready")
        wo_s = sem("out_rows")
        res = sem("residual_added")
        h2_turned = sem("h2_turned")
        h2h, h2l = sem("h2_hi_ready"), sem("h2_lo_ready")
        silu_s, gated_s = sem("silu_ready"), sem("gated_ready")
        ah_s, al_s = sem("hidden_hi_ready"), sem("hidden_lo_ready")
        y_done = sem("down_rows")
        y_add = sem("output_added")
        stored = sem("stored")

        def turned(t, qt, a):
            if t < MOBA_PAIRS:
                return 8 * t + 2 * qt + a + 1
            return 8 * MOBA_PAIRS + 4 * (t - MOBA_PAIRS) + qt + 1

        def used(g):
            return g + 1 if g < G_OUT else g + 1 - KT

        block = ctx.enter_context(nc.Block())

        @block.sync
        def _(sp):
            def load(g):
                if g >= 28:
                    sp.wait_ge(w_lo, g - 3)
                elif 3 <= g < 27:
                    sp.wait_ge(w_lo, g - 2)
                s = raw_slot(g)
                sp.dma_start(RAW[:, s], wt[g]).then_inc(raw_in[s], 16)

            def rotate(dst, src, evac, pool, done, p):
                sp.wait_ge(evac, 2 * p + 2)
                if p >= 1:
                    sp.wait_ge(pool, 3 * p)
                for b in range(4):
                    sp.dma_start(dst[32 * b:32 * b + 32], src[32 * (b ^ 1):32 * (b ^ 1) + 32]).then_inc(done, 16)

            for t in range(TT):
                sp.dma_start(X[:, t], x[t]).then_inc(x_in[t], 16)
                if t == 0:
                    sp.dma_start(ident[:], ident_in).then_inc(ident_in_s, 16)
                    sp.dma_start(small[:, 0:16], vec).then_inc(small_in, 16)
                    sp.dma_start(small[:, 16:18], ind_in).then_inc(small_in, 16)
            load(0)
            sp.dma_start(MASK0[:], mask_in).then_inc(misc_in, 16)
            sp.dma_start(LAM0[:], lams).then_inc(misc_in, 16)
            load(1)
            sp.dma_start(cosT[:], cos_in).then_inc(rope_in, 16)
            sp.dma_start(sinT[:], sin_in).then_inc(rope_in, 16)
            load(2)
            for p in range(PAIRS):
                load(3 * p + 3)
                rotate(QR, QG, q_ev, q_pool, q_rot, p)
                load(3 * p + 4)
                rotate(KR, KG, k_ev, k_pool, k_rot, p)
                load(3 * p + 5)
            for g in range(27, 32):
                load(g)
            sp.wait_ge(pv_s, PAIRS)
            sp.dma_start(G2[:], gain2).then_inc(gain2_in, 16)
            for g in range(32, TILES):
                load(g)
            for tt in range(TT):
                for half in range(2):
                    sp.wait_ge(y_add, 2 * tt + half + 1)
                    sp.dma_start(out[tt, :, half * SEQ:(half + 1) * SEQ],
                                 X[:, tt, half * SEQ:(half + 1) * SEQ]).then_inc(stored, 16)
            sp.wait_ge(stored, 16 * 2 * TT)

        @block.gpsimd
        def _(pool):
            def rope(p, G, R, S, rot, step, hi, lo):
                pool.wait_ge(rot, 64 * (p + 1))
                if p >= 1:
                    pool.wait_ge(hi, p)
                    pool.wait_ge(lo, p)
                nc.gpsimd.tensor_tensor(G[:], G[:], cosT[:], ALU.mult).then_inc(step, 1)
                nc.gpsimd.tensor_tensor(R[:], R[:], sinT[:], ALU.mult).then_inc(step, 1)
                pool.wait_ge(step, 3 * p + 2)
                nc.gpsimd.tensor_tensor(S[:], G[:], R[:], ALU.add).then_inc(step, 1)

            pool.wait_ge(rope_in, 32)
            for p in range(PAIRS):
                rope(p, QG, QR, QS, q_rot, q_pool, qh_s, ql_s)
                rope(p, KG, KR, KS, k_rot, k_pool, kh_s, kl_s)

        @block.scalar
        def _(act):
            def split_hi(g):
                act.wait_ge(raw_in[raw_slot(g)], 16 * raw_loads(g))
                if g < 27:
                    if g >= 3:
                        act.wait_ge(w_used, g - 2)
                    dst = WH[:, g % 3]
                elif g < 31:
                    act.wait_ge(w_used, G_OUT)
                    dst = HH[:, 2 * (g - 27):2 * (g - 27) + 2, :].rearrange("p k n -> p (k n)")
                else:
                    if g == 31:
                        act.wait_ge(pt_s, turned(PAIRS - 1, TT - 1, 1))
                    else:
                        if g < G_FFN + 4:
                            act.wait_ge(wo_s, TT)
                        else:
                            act.wait_ge(w_used, used(g - 4))
                    dst = WH[:, g % 4]
                nc.scalar.activation(dst, RAW[:, raw_slot(g)], ACT.Copy).then_inc(w_hi, 1)

            def evacuate(p, j, bank, SQ, G, ev, col, evs):
                act.wait_ge(w_used, 3 * p + j + 1)
                if p >= 1:
                    act.wait_ge(ms_s, p)
                if p > MOBA_PAIRS + 1:
                    act.wait_ge(o_sq, p - MOBA_PAIRS - 1)
                nc.scalar.activation(SQ[:], ps[:, bank], ACT.Square).then_inc(ev, 1)
                if p >= 1:
                    act.wait_ge(evs, 3 * p)
                nc.scalar.activation(G[:], ps[:, bank], ACT.Copy, scale=VEC[:, col:col + 1]).then_inc(ev, 1)

            def q_evac(p):
                evacuate(p, 0, 0, SQQ, QG, q_ev, 8 if p < MOBA_PAIRS else 10, q_pool)

            def k_evac(p):
                evacuate(p, 1, 1, SQK, KG, k_ev, 9 if p < MOBA_PAIRS else 11, k_pool)

            def v_evac(p):
                act.wait_ge(w_used, 3 * p + 3)
                if p >= 1:
                    act.wait_ge(v_turn, p)
                nc.scalar.activation(VT[:], ps[:, 0], ACT.Copy).then_inc(v_ev, 1)

            def q_hi(p):
                act.wait_ge(q_pool, 3 * p + 3)
                if p >= 1:
                    act.wait_ge(sc_s, 8 * p)
                nc.scalar.activation(QH[:], QS[:], ACT.Copy).then_inc(qh_s, 1)

            def k_hi(p):
                act.wait_ge(kn_s, p + 1)
                if p >= 1:
                    act.wait_ge(sc_s, 8 * p)
                nc.scalar.activation(KH[:], KS[:], ACT.Copy).then_inc(kh_s, 1)

            def v_hi(t):
                act.wait_ge(v_turn, t + 1)
                act.wait_ge(pads, 1)
                if t >= 1:
                    act.wait_ge(pv_s, t)
                turned_v = ps[:, 7].rearrange("p (t d) -> p t d", t=TT)
                if t < MOBA_PAIRS:
                    nc.scalar.activation(VH[:, 0, :, 0:HEAD], turned_v[:, :, 0:HEAD], ACT.Copy)
                    nc.scalar.activation(VH[:, 1, :, HEAD:P], turned_v[:, :, HEAD:P], ACT.Copy).then_inc(vh_s, 1)
                else:
                    nc.scalar.activation(VH[:, 0], turned_v, ACT.Copy).then_inc(vh_s, 1)

            def exps(t, qt):
                W = (qt + 1) * P
                for a in range(2):
                    i = 2 * qt + a
                    act.wait_ge(nb_s, 8 * t + i + 1)
                    if t >= 1 or qt >= 2:
                        before = (t, qt - 2) if qt >= 2 else (t - 1, qt + 2)
                        act.wait_ge(pt_s, turned(before[0], before[1], a if before[0] < MOBA_PAIRS else 1))
                    nc.scalar.activation(PR[qt % 2][:, a, 0:W], ps[:, 2 + a, 0:W], ACT.Exp, bias=NB[:, i:i + 1],
                                         scale=RQ[:, i:i + 1], accum_out=SUM[:, i:i + 1]).then_inc(ex_s, 1)

            def maps(t):
                return range(2) if t < MOBA_PAIRS else range(1)

            def pt_hi(t, qt):
                for a in maps(t):
                    act.wait_ge(pt_s, turned(t, qt, a))
                    if t >= 1:
                        act.wait_ge(pv_s, t)
                    bank = 4 + (a if t < MOBA_PAIRS else qt % 2)
                    nc.scalar.activation(PTH[:, a, 0:qt + 1, qt * P:(qt + 1) * P],
                                         ps[:, bank, 0:(qt + 1) * P].rearrange("p (k q) -> p k q", q=P),
                                         ACT.Copy).then_inc(ph_s, 1)

            def o_squares(t):
                act.wait_ge(pv_s, t + 1)
                act.wait_ge(ms_s, min(t + 2, PAIRS))
                for qt in range(TT):
                    qs = slice(qt * P, (qt + 1) * P)
                    ins = nc.scalar.activation(SQQ[:, qs], ps[:, 6, qs], ACT.Square, accum_out=SO[:, qt:qt + 1])
                ins.then_inc(o_sq, 1)

            def mix_hi(t):
                if t < MOBA_PAIRS:
                    act.wait_ge(pv_s, t + 1)
                    nc.scalar.activation(MH[:, t], ps[:, 6], ACT.Copy).then_inc(mh_s, 1)
                else:
                    act.wait_ge(o_turn, t - MOBA_PAIRS + 1)
                    nc.scalar.activation(MH[:, t], ps[:, 6], ACT.Copy, scale=SUBG).then_inc(mh_s, 1)

            for t in range(TT):
                act.wait_ge(x_in[t], 16)
                if t >= 1:
                    act.wait_ge(x_sq, t)
                nc.scalar.activation(JUNK[:], X[:, t], ACT.Square, accum_out=SS[:, t:t + 1]).then_inc(x_sq, 1)
            split_hi(0)
            act.wait_ge(ident_in_s, 16)
            nc.scalar.activation(identR[:], ident[:], ACT.Copy).then_inc(consts, 1)
            act.wait_ge(small_in, 32)
            for k in range(KT):
                act.wait_ge(x_turned, k + 1)
                nc.scalar.activation(HH[:, k], ps[:, k], ACT.Copy, scale=VEC[:, k:k + 1]).then_inc(hh, 1)
            split_hi(1)
            act.wait_ge(misc_in, 32)
            nc.scalar.activation(maskR[:], MASK0[:], ACT.Copy).then_inc(consts, 1)
            act.wait_ge(lam_dot, 2)
            nc.scalar.activation(LP[:, 2:4], LP[:, 0:2], ACT.Exp).then_inc(lam_exp, 1)
            split_hi(2)
            q_evac(0)
            split_hi(3)
            k_evac(0)
            split_hi(4)
            q_hi(0)
            k_hi(0)
            v_evac(0)
            for t in range(PAIRS):
                p = t + 1
                more = p < PAIRS
                split_hi(3 * p + 2)
                if t > MOBA_PAIRS:
                    o_squares(t - 1)
                v_hi(t)
                exps(t, 0)
                if t > MOBA_PAIRS:
                    mix_hi(t - 1)
                exps(t, 1)
                if more:
                    q_evac(p)
                split_hi(3 * (p + 1) if more else 27)
                exps(t, 2)
                pt_hi(t, 0)
                exps(t, 3)
                pt_hi(t, 1)
                pt_hi(t, 2)
                if more:
                    q_hi(p)
                else:
                    split_hi(28)
                pt_hi(t, 3)
                if more:
                    k_evac(p)
                    split_hi(3 * (p + 1) + 1)
                else:
                    split_hi(29)
                if t < MOBA_PAIRS:
                    mix_hi(t)
                if more:
                    k_hi(p)
                    v_evac(p)
            split_hi(30)
            split_hi(31)
            o_squares(PAIRS - 1)
            mix_hi(PAIRS - 1)
            for tt in range(TT + 1):
                if tt < TT:
                    act.wait_ge(res, 2 * tt + 2)
                    act.wait_ge(x_sq, TT + tt)
                    nc.scalar.activation(JUNK[:], X[:, tt], ACT.Square, accum_out=S2[:, tt:tt + 1]).then_inc(x_sq, 1)
                if tt >= 1:
                    act.wait_ge(h2_turned, tt)
                    if tt == 1:
                        act.wait_ge(wo_s, TT)
                    b = 4 + 2 * ((tt - 1) % 2)
                    nc.scalar.activation(HH[:, :, (tt - 1) * P:tt * P],
                                         ps[:, b:b + 2].rearrange("p b (k q) -> p (b k) q", q=P),
                                         ACT.Copy).then_inc(h2h, 1)
            for g in range(G_FFN, G_FFN + 4):
                split_hi(g)

            def silu(f):
                act.wait_ge(w_used, used(G_FFN + 2 * f))
                if f >= 2:
                    act.wait_ge(gated_s, f - 1)
                nc.scalar.activation(SG[:, f % 2], ps[:, 2 * (f % 2)], ACT.Silu).then_inc(silu_s, 1)

            def hidden_hi(f):
                act.wait_ge(gated_s, f + 1)
                nc.scalar.activation(AH[:, f], AC[:, f % 2], ACT.Copy).then_inc(ah_s, 1)

            for f in range(FT):
                silu(f)
                g = G_FFN + 2 * f + 4
                if g < TILES:
                    split_hi(g)
                hidden_hi(f)
                if g + 1 < TILES:
                    split_hi(g + 1)
            for g in range(G_DOWN + 4, TILES):
                split_hi(g)

        @block.vector
        def _(dve):
            steps = [0]

            def step(ins):
                steps[0] += 1
                ins.then_inc(newton, 1)
                dve.wait_ge(newton, steps[0])

            def rsqrt(src, n, scale, at=0):
                a, h, y, z = (v[:, 0:n] for v in (NA, NT, NY, NZ))
                step(nc.vector.tensor_scalar(a, src, scale, EPS, ALU.mult, ALU.add))
                step(nc.vector.tensor_scalar(h.bitcast(U32), a.bitcast(U32), 1, None, ALU.logical_shift_right))
                step(nc.vector.tensor_scalar(y.bitcast(U32), h.bitcast(U32), -1.0, float(RSQRT_MAGIC),
                                             ALU.mult, ALU.add))
                for _ in range(NEWTON):
                    step(nc.vector.tensor_tensor(z, y, y, ALU.mult))
                    step(nc.vector.scalar_tensor_tensor(out=z, in0=z, scalar=-0.5, in1=a, op0=ALU.mult, op1=ALU.mult))
                    step(nc.vector.scalar_tensor_tensor(out=y, in0=z, scalar=1.5, in1=y, op0=ALU.add, op1=ALU.mult))
                return y

            def split_lo(g):
                dve.wait_ge(w_hi, g + 1)
                if g < 27:
                    hi, lo = WH[:, g % 3], WL[:, g % 3]
                elif g < 31:
                    hi, lo = (v[:, 2 * (g - 27):2 * (g - 27) + 2, :].rearrange("p k n -> p (k n)") for v in (HH, HL))
                else:
                    hi, lo = WH[:, g % 4], WL[:, g % 4]
                nc.vector.tensor_tensor(lo, RAW[:, raw_slot(g)], hi.bitcast(F32), ALU.subtract).then_inc(w_lo, 1)

            def q_lo(p):
                dve.wait_ge(qh_s, p + 1)
                nc.vector.tensor_tensor(QL[:], QS[:], QH[:].bitcast(F32), ALU.subtract).then_inc(ql_s, 1)

            def scales(p):
                dve.wait_ge(ms_s, p + 1)
                y = rsqrt(ps[:, 7, 0:16], 16, 1.0)
                if p >= 1:
                    dve.wait_ge(ex_s, 8 * p)
                nc.vector.tensor_scalar(RQ, y[:, 0:8], HEAD ** -0.5, None, ALU.mult).then_inc(rq_s, 1)
                if p >= 1:
                    dve.wait_ge(kb_s, p)
                nc.vector.tensor_copy(KBC[:].rearrange("p t a e -> p (t a) e"),
                                      y[:, 8:16].unsqueeze(2).broadcast_to([P, 8, HEAD])).then_inc(kbc_s, 1)

            def k_norm(p):
                dve.wait_ge(kb_s, p + 1)
                dve.wait_ge(k_pool, 3 * p + 3)
                nc.vector.tensor_tensor(KS[:], KS[:], ps[:, 7], ALU.mult).then_inc(kn_s, 1)
                dve.wait_ge(kh_s, p + 1)
                nc.vector.tensor_tensor(KL[:], KS[:], KH[:].bitcast(F32), ALU.subtract).then_inc(kl_s, 1)

            def v_lo(t):
                dve.wait_ge(vh_s, t + 1)
                turned_v = ps[:, 7].rearrange("p (t d) -> p t d", t=TT)
                if t < MOBA_PAIRS:
                    nc.vector.tensor_tensor(VL[:, 0, :, 0:HEAD], turned_v[:, :, 0:HEAD],
                                            VH[:, 0, :, 0:HEAD].bitcast(F32), ALU.subtract)
                    nc.vector.tensor_tensor(VL[:, 1, :, HEAD:P], turned_v[:, :, HEAD:P],
                                            VH[:, 1, :, HEAD:P].bitcast(F32), ALU.subtract).then_inc(vl_s, 1)
                else:
                    nc.vector.tensor_tensor(VL[:, 0], turned_v, VH[:, 0].bitcast(F32), ALU.subtract).then_inc(vl_s, 1)

            def maxima(t, qt):
                W = (qt + 1) * P
                for a in range(2):
                    i = 2 * qt + a
                    dve.wait_ge(sc_s, 8 * t + i + 1)
                    nc.vector.tensor_reduce(MX[:, i:i + 1], ps[:, 2 + a, 0:W], AX.X, ALU.max).then_inc(mx_s, 1)
                for a in range(2):
                    i = 2 * qt + a
                    dve.wait_ge(mx_s, 8 * t + i + 1)
                    dve.wait_ge(rq_s, t + 1)
                    nc.vector.scalar_tensor_tensor(out=NB[:, i:i + 1], in0=MX[:, i:i + 1], scalar=-1.0,
                                                   in1=RQ[:, i:i + 1], op0=ALU.mult, op1=ALU.mult).then_inc(nb_s, 1)

            def norm(t, qt):
                W = (qt + 1) * P
                i = 2 * qt
                p0, p1 = PR[qt % 2][:, 0, 0:W], PR[qt % 2][:, 1, 0:W]
                dve.wait_ge(ex_s, 8 * t + i + 2)
                nc.vector.reciprocal(RS[:, i:i + 2], SUM[:, i:i + 2]).then_inc(rs_s, 1)
                dve.wait_ge(rs_s, 4 * t + qt + 1)
                if t < MOBA_PAIRS:
                    nc.vector.tensor_scalar(p0, p0, RS[:, i:i + 1], None, ALU.mult).then_inc(pn_s, 1)
                    nc.vector.tensor_scalar(p1, p1, RS[:, i + 1:i + 2], None, ALU.mult).then_inc(pn_s, 1)
                else:
                    n = 2 * (4 * (t - MOBA_PAIRS) + qt)
                    nc.vector.tensor_tensor(NL[:, qt:qt + 1], RS[:, i + 1:i + 2], LAM, ALU.mult).then_inc(lr_s, 1)
                    dve.wait_ge(lr_s, n + 1)
                    nc.vector.tensor_scalar(p1, p1, NL[:, qt:qt + 1], None, ALU.mult).then_inc(lr_s, 1)
                    dve.wait_ge(lr_s, n + 2)
                    nc.vector.scalar_tensor_tensor(out=p0, in0=p0, scalar=RS[:, i:i + 1], in1=p1,
                                                   op0=ALU.mult, op1=ALU.subtract).then_inc(pn_s, 1)

            def pt_lo(t, qt):
                for a in (range(2) if t < MOBA_PAIRS else range(1)):
                    dve.wait_ge(ph_s, turned(t, qt, a))
                    bank = 4 + (a if t < MOBA_PAIRS else qt % 2)
                    at = (slice(None), a, slice(0, qt + 1), slice(qt * P, (qt + 1) * P))
                    nc.vector.tensor_tensor(PTL[at], ps[:, bank, 0:(qt + 1) * P].rearrange("p (k q) -> p k q", q=P),
                                            PTH[at].bitcast(F32), ALU.subtract).then_inc(pl_s, 1)

            def o_norm(t):
                dve.wait_ge(o_sq, t - MOBA_PAIRS + 1)
                y = rsqrt(SO, 4, 1.0 / P)
                for qt in range(TT):
                    ins = nc.vector.tensor_scalar(ON[:, qt], ps[:, 6, qt * P:(qt + 1) * P], y[:, qt:qt + 1], None,
                                                  ALU.mult)
                ins.then_inc(on_s, 1)

            def mix_lo(t):
                dve.wait_ge(mh_s, t + 1)
                if t < MOBA_PAIRS:
                    nc.vector.tensor_tensor(ML[:, t], ps[:, 6], MH[:, t].bitcast(F32), ALU.subtract).then_inc(ml_s, 1)
                else:
                    nc.vector.scalar_tensor_tensor(out=ML[:, t], in0=ps[:, 6], scalar=SUBG, in1=MH[:, t].bitcast(F32),
                                                   op0=ALU.mult, op1=ALU.subtract).then_inc(ml_s, 1)

            dve.wait_ge(x_sq, TT)
            y = rsqrt(SS, TT, 1.0 / D)
            for t in range(TT):
                nc.vector.tensor_scalar(HN[:, t], X[:, t], y[:, t:t + 1], None, ALU.mult).then_inc(hn, 1)
            split_lo(0)
            dve.wait_ge(small_in, 32)
            for k in range(KT):
                dve.wait_ge(hh, k + 1)
                nc.vector.scalar_tensor_tensor(out=HL[:, k], in0=ps[:, k], scalar=VEC[:, k:k + 1],
                                               in1=HH[:, k].bitcast(F32), op0=ALU.mult, op1=ALU.subtract).then_inc(hl, 1)
            split_lo(1)
            dve.wait_ge(misc_in, 32)
            for j in range(2):
                step(nc.vector.tensor_tensor(LAM0[:, 2 * j * HEAD:(2 * j + 1) * HEAD],
                                             LAM0[:, 2 * j * HEAD:(2 * j + 1) * HEAD],
                                             LAM0[:, (2 * j + 1) * HEAD:(2 * j + 2) * HEAD], ALU.mult))
                nc.vector.tensor_reduce(LP[:, j:j + 1], LAM0[:, 2 * j * HEAD:(2 * j + 1) * HEAD], AX.X,
                                        ALU.add).then_inc(lam_dot, 1)
            nc.vector.memset(VH[:, 0, :, HEAD:P].bitcast(F32), 0.0)
            nc.vector.memset(VH[:, 1, :, 0:HEAD].bitcast(F32), 0.0)
            nc.vector.memset(VL[:, 0, :, HEAD:P].bitcast(F32), 0.0)
            nc.vector.memset(VL[:, 1, :, 0:HEAD].bitcast(F32), 0.0).then_inc(pads, 1)
            nc.vector.tensor_scalar(SUBG, VEC[:, 12:13], 1.0 - LAMBDA_INIT, None, ALU.mult)
            dve.wait_ge(lam_exp, 1)
            step(nc.vector.tensor_tensor(LAM, LP[:, 2:3], LP[:, 3:4], ALU.subtract))
            nc.vector.tensor_scalar(LAM, LAM, LAMBDA_INIT, None, ALU.add).then_inc(lam_s, 1)
            split_lo(2)
            split_lo(3)
            split_lo(4)
            q_lo(0)
            scales(0)
            k_norm(0)
            dve.wait_ge(lam_s, 1)
            for t in range(PAIRS):
                p = t + 1
                more = p < PAIRS
                split_lo(3 * p + 2)
                if t > MOBA_PAIRS:
                    o_norm(t - 1)
                v_lo(t)
                maxima(t, 0)
                if t > MOBA_PAIRS:
                    mix_lo(t - 1)
                maxima(t, 1)
                norm(t, 0)
                split_lo(3 * (p + 1) if more else 27)
                maxima(t, 2)
                norm(t, 1)
                pt_lo(t, 0)
                maxima(t, 3)
                norm(t, 2)
                pt_lo(t, 1)
                norm(t, 3)
                pt_lo(t, 2)
                if more:
                    q_lo(p)
                else:
                    split_lo(28)
                pt_lo(t, 3)
                split_lo(3 * (p + 1) + 1 if more else 29)
                if more:
                    scales(p)
                if t < MOBA_PAIRS:
                    mix_lo(t)
                if more:
                    k_norm(p)
            split_lo(30)
            split_lo(31)
            o_norm(PAIRS - 1)
            mix_lo(PAIRS - 1)
            dve.wait_ge(gain2_in, 16)

            def h2_lo(tt):
                dve.wait_ge(h2h, tt + 1)
                b = 4 + 2 * (tt % 2)
                at = (slice(None), slice(None), slice(tt * P, (tt + 1) * P))
                nc.vector.tensor_tensor(HL[at], ps[:, b:b + 2].rearrange("p b (k q) -> p (b k) q", q=P),
                                        HH[at].bitcast(F32), ALU.subtract).then_inc(h2l, 1)

            for tt in range(TT):
                dve.wait_ge(wo_s, tt + 1)
                for half in range(2):
                    at = (slice(None), tt, slice(half * SEQ, (half + 1) * SEQ))
                    nc.vector.tensor_tensor(X[at], ps[:, 2 * (tt % 2) + half], X[at], ALU.add).then_inc(res, 1)
                dve.wait_ge(x_sq, TT + tt + 1)
                y = rsqrt(S2[:, tt:tt + 1], 1, 1.0 / D)
                nc.vector.scalar_tensor_tensor(out=HN[:, tt], in0=X[:, tt], scalar=y, in1=G2[:], op0=ALU.mult,
                                               op1=ALU.mult).then_inc(hn, 1)
                if tt == TT - 1:
                    for u in range(TT - 1):
                        h2_lo(u)
            h2_lo(TT - 1)
            for g in range(G_FFN, G_FFN + 4):
                split_lo(g)
            for f in range(FT):
                dve.wait_ge(silu_s, f + 1)
                dve.wait_ge(w_used, used(G_FFN + 2 * f + 1))
                if f >= 2:
                    dve.wait_ge(ah_s, f - 1)
                    dve.wait_ge(al_s, f - 1)
                nc.vector.tensor_tensor(AC[:, f % 2], ps[:, 2 * (f % 2) + 1], SG[:, f % 2], ALU.mult).then_inc(gated_s, 1)
                g = G_FFN + 2 * f + 4
                if g < TILES:
                    split_lo(g)
                dve.wait_ge(ah_s, f + 1)
                nc.vector.tensor_tensor(AL[:, f], AC[:, f % 2], AH[:, f].bitcast(F32), ALU.subtract).then_inc(al_s, 1)
                if g + 1 < TILES:
                    split_lo(g + 1)
            for g in range(G_DOWN + 4, TILES):
                split_lo(g)
            for tt in range(TT):
                for half in range(2):
                    dve.wait_ge(y_done, 2 * tt + half + 1)
                    at = (slice(None), tt, slice(half * SEQ, (half + 1) * SEQ))
                    nc.vector.tensor_tensor(X[at], ps[:, 2 * tt + half], X[at], ALU.add).then_inc(y_add, 1)

        @block.tensor
        def _(pe):
            def product(dst, lh, ll, rh, rl, start, stop):
                nc.tensor.matmul(dst, lh, rh, start=start, stop=False, skip_group_check=True)
                nc.tensor.matmul(dst, lh, rl, start=False, stop=False, skip_group_check=True)
                return nc.tensor.matmul(dst, ll, rh, start=False, stop=stop, skip_group_check=True)

            def project(p, n):
                j, k = divmod(n, KT)
                g = 3 * p + j
                if k == 0:
                    pe.wait_ge(w_hi, g + 1)
                    pe.wait_ge(w_lo, g + 1)
                    if j == 0 and p >= 1:
                        pe.wait_ge(v_ev, p)
                    if j == 1 and p >= 1:
                        pe.wait_ge(k_ev, 2 * p)
                    if j == 2:
                        pe.wait_ge(q_ev, 2 * p + 2)
                if g == 0:
                    pe.wait_ge(hh, k + 1)
                    pe.wait_ge(hl, k + 1)
                w = slice(k * P, (k + 1) * P)
                ins = product(ps[:, j % 2], WH[:, j, w], WL[:, j, w], HH[:, k], HL[:, k], k == 0, k == KT - 1)
                if k == KT - 1:
                    ins.then_inc(w_used, 1)

            def mean_squares(p):
                pe.wait_ge(k_ev, 2 * p + 1)
                if p >= 1:
                    pe.wait_ge(vl_s, p)
                for j, SQ in enumerate((SQQ, SQK)):
                    for tt in range(TT):
                        c = 2 * (TT * j + tt)
                        ins = nc.tensor.matmul(ps[:, 7, c:c + 2], SQ[:, tt * P:(tt + 1) * P], IND, start=True, stop=True,
                                               skip_group_check=True)
                ins.then_inc(ms_s, 1)

            def spread_k(p):
                pe.wait_ge(kbc_s, p + 1)
                for tt in range(TT):
                    ins = nc.tensor.transpose(ps[:, 7, tt * P:(tt + 1) * P],
                                              KBC[:, tt].rearrange("p a e -> p (a e)"), ident[:])
                ins.then_inc(kb_s, 1)

            def turn_v(t):
                pe.wait_ge(v_ev, t + 1)
                pe.wait_ge(kn_s, t + 1)
                for tt in range(TT):
                    ins = nc.tensor.transpose(ps[:, 7, tt * P:(tt + 1) * P], VT[:, tt * P:(tt + 1) * P], ident[:])
                ins.then_inc(v_turn, 1)

            def scores(t, qt):
                W = (qt + 1) * P
                qs = slice(qt * P, W)
                if qt == 0:
                    for s in (qh_s, ql_s, kh_s, kl_s):
                        pe.wait_ge(s, t + 1)
                if t >= 1 or qt >= 1:
                    pe.wait_ge(ex_s, 8 * t + 2 * qt)
                rows = (slice(0, HEAD), slice(HEAD, P))
                for left, right, first in ((QH, KH, True), (QH, KL, False), (QL, KH, False)):
                    for a in range(2):
                        nc.tensor.matmul(ps[:, 2 + a, 0:W], left[rows[a], qs], right[rows[a], 0:W], start=first,
                                         stop=False, skip_group_check=True)
                pe.wait_ge(consts, 2)
                for a in range(2):
                    nc.tensor.matmul(ps[:, 2 + a, qs], identR[:], maskR[:], start=False, stop=True,
                                     skip_group_check=True).then_inc(sc_s, 1)

            def turn_p(t, qt):
                for a in (range(2) if t < MOBA_PAIRS else range(1)):
                    n = turned(t, qt, a)
                    pe.wait_ge(pn_s, n)
                    if n > 2:
                        pe.wait_ge(pl_s, n - 2)
                    bank = 4 + (a if t < MOBA_PAIRS else qt % 2)
                    for kt in range(qt + 1):
                        ins = nc.tensor.transpose(ps[:, bank, kt * P:(kt + 1) * P],
                                                  PR[qt % 2][:, a, kt * P:(kt + 1) * P], ident[:])
                    ins.then_inc(pt_s, 1)

            def heads_out(t, part):
                if part == 0:
                    pe.wait_ge(pl_s, turned(t, TT - 1, 1))
                    pe.wait_ge(vh_s, t + 1)
                    pe.wait_ge(vl_s, t + 1)
                    if t >= 1:
                        pe.wait_ge(ml_s, t)
                if t < MOBA_PAIRS:
                    for kt in range(TT):
                        ins = product(ps[:, 6, kt * P:SEQ], VH[:, part, kt], VL[:, part, kt],
                                      PTH[:, part, kt, kt * P:SEQ], PTL[:, part, kt, kt * P:SEQ],
                                      part == 0 and kt == 0, part == 1 and kt == TT - 1)
                else:
                    for qt in ((0, 1, 2), (3,))[part]:
                        for kt in range(qt + 1):
                            qs = slice(qt * P, (qt + 1) * P)
                            ins = product(ps[:, 6, qs], PTH[:, 0, kt, qs], PTL[:, 0, kt, qs], VH[:, 0, kt], VL[:, 0, kt],
                                          kt == 0, kt == qt)
                if part == 1:
                    ins.then_inc(pv_s, 1)

            def turn_o(t):
                pe.wait_ge(on_s, t - MOBA_PAIRS + 1)
                for qt in range(TT):
                    ins = nc.tensor.transpose(ps[:, 6, qt * P:(qt + 1) * P], ON[:, qt], ident[:])
                ins.then_inc(o_turn, 1)

            def w_out_parts(k):
                if 3 <= k < 7:
                    return [(HH[:, 2 * (k - 3) + h], HL[:, 2 * (k - 3) + h]) for h in range(2)]
                return [(WH[:, k % 4, h * SEQ:(h + 1) * SEQ], WL[:, k % 4, h * SEQ:(h + 1) * SEQ]) for h in range(2)]

            def w_out(tt, k):
                pe.wait_ge(w_lo, G_OUT + k + 1)
                pe.wait_ge(ml_s, k + 1)
                qs = slice(tt * P, (tt + 1) * P)
                for h, (wh, wl) in enumerate(w_out_parts(k)):
                    ins = product(ps[:, 2 * (tt % 2) + h], MH[:, k, qs], ML[:, k, qs], wh, wl, k == 0, k == KT - 1)
                return ins

            pe.wait_ge(ident_in_s, 16)
            for tt in range(TT):
                pe.wait_ge(hn, tt + 1)
                for k in range(KT):
                    ins = nc.tensor.transpose(ps[:, k, tt * P:(tt + 1) * P], HN[:, tt, k * P:(k + 1) * P], ident[:])
                    if tt == TT - 1:
                        ins.then_inc(x_turned, 1)
            for n in range(18):
                project(0, n)
            pe.wait_ge(hl, KT)
            mean_squares(0)
            for n in range(18, 22):
                project(0, n)
            spread_k(0)
            for n in range(22, 24):
                project(0, n)
            for t in range(PAIRS):
                p = t + 1
                done = [0]

                def fill(n):
                    for _ in range(n):
                        m = done[0]
                        done[0] += 1
                        if p < PAIRS:
                            project(p, m)
                        elif m % 3 == 2 and m // 3 < 7:
                            if m == 2:
                                pe.wait_ge(v_ev, PAIRS)
                                pe.wait_ge(k_ev, 2 * PAIRS)
                            w_out(0, m // 3)

                fill(3)
                if t > MOBA_PAIRS:
                    turn_o(t - 1)
                turn_v(t)
                fill(1)
                scores(t, 0)
                fill(2)
                scores(t, 1)
                fill(2)
                scores(t, 2)
                fill(1)
                turn_p(t, 0)
                fill(1)
                scores(t, 3)
                fill(1)
                turn_p(t, 1)
                fill(2)
                turn_p(t, 2)
                fill(2)
                turn_p(t, 3)
                fill(1)
                heads_out(t, 0)
                fill(1)
                if p < PAIRS:
                    mean_squares(p)
                heads_out(t, 1)
                fill(5)
                if p < PAIRS:
                    spread_k(p)
                fill(2)
            turn_o(PAIRS - 1)
            def turn_h2(tt):
                pe.wait_ge(hn, TT + tt + 1)
                if tt >= 2:
                    pe.wait_ge(h2l, tt - 1)
                for k in range(KT):
                    b = 4 + 2 * (tt % 2) + k // 4
                    ins = nc.tensor.transpose(ps[:, b, (k % 4) * P:(k % 4 + 1) * P], HN[:, tt, k * P:(k + 1) * P],
                                              ident[:])
                ins.then_inc(h2_turned, 1)

            for tt in range(TT):
                if tt >= 2:
                    pe.wait_ge(res, 2 * tt - 2)
                for k in range(7 if tt == 0 else 0, KT):
                    ins = w_out(tt, k)
                    if k == KT - 1:
                        ins.then_inc(wo_s, 1)
            for k in range(KT):
                pass
            for tt in range(TT):
                turn_h2(tt)
            for f in range(FT):
                for j in range(2):
                    g = G_FFN + 2 * f + j
                    pe.wait_ge(w_lo, g + 1)
                    if f == 0 and j == 0:
                        pe.wait_ge(h2l, TT)
                    if f >= 2:
                        pe.wait_ge((silu_s, gated_s)[j], f - 1)
                    for k in range(KT):
                        w = slice(k * P, (k + 1) * P)
                        ins = product(ps[:, 2 * (f % 2) + j], WH[:, g % 4, w], WL[:, g % 4, w], HH[:, k], HL[:, k],
                                      k == 0, k == KT - 1)
                    ins.then_inc(w_used, 1)

            def down(f, tt, half):
                s = (G_DOWN + f) % 4
                qs, cs = slice(tt * P, (tt + 1) * P), slice(half * SEQ, (half + 1) * SEQ)
                return product(ps[:, 2 * tt + half], AH[:, f, qs], AL[:, f, qs], WH[:, s, cs], WL[:, s, cs],
                               f == 0, f == FT - 1)

            TAIL = 3
            for f in range(FT - TAIL):
                pe.wait_ge(w_lo, G_DOWN + f + 1)
                pe.wait_ge(al_s, f + 1)
                for tt in (2, 3, 0, 1):
                    if f == 0 and tt == 0:
                        pe.wait_ge(gated_s, FT)
                    for half in range(2):
                        ins = down(f, tt, half)
                ins.then_inc(w_used, 1)
            pe.wait_ge(w_lo, TILES)
            pe.wait_ge(al_s, FT)
            for tt in range(TT):
                for half in range(2):
                    for f in range(FT - TAIL, FT):
                        ins = down(f, tt, half)
                    ins.then_inc(y_done, 1)


def kernel(**inputs):
    import numpy as _np
    import concourse.bacc as _bacc
    from concourse import mybir as _mybir
    from concourse.bass_utils import run_bass_kernel_spmd as _run

    a = {k: _np.ascontiguousarray(v) for k, v in inputs.items()}
    f32 = _np.float32

    def columns(w, c):
        return w[:, c:c + P].reshape(KT, P, P).transpose(1, 0, 2).reshape(P, D)

    w_in = a["w_in"][0]
    tiles = []
    for p in range(PAIRS):
        base, n = (0, p) if p < MOBA_PAIRS else (3 * MOBA_PAIRS * P, p - MOBA_PAIRS)
        for j in range(3):
            tiles.append(columns(w_in, base + (j * MOBA_PAIRS + n) * P))
    for k in range(KT):
        tiles.append(a["w_out"][0][k * P:(k + 1) * P])
    for f in range(FT):
        tiles.append(columns(a["w_gate"][0], f * P))
        tiles.append(columns(a["w_up"][0], f * P))
    for f in range(FT):
        tiles.append(a["w_down"][0][f * P:(f + 1) * P])

    vec = _np.zeros((P, 16), f32)
    vec[:, 0:8] = a["attn_norm"][0].reshape(KT, P).T
    for c, name in enumerate(("moba_q_norm", "moba_k_norm", "diff_q_norm", "diff_k_norm")):
        vec[:, 8 + c] = _np.tile(a[name][0], 2)
    vec[:, 12] = a["diff_subln"][0]
    lams = _np.concatenate([a[n][0] for n in ("lambda_q1", "lambda_k1", "lambda_q2", "lambda_k2")])

    inv = (1.0 / (f32(10000.0) ** (_np.arange(0, HEAD, 2, dtype=f32) / f32(HEAD)))).astype(f32)
    ang = _np.arange(SEQ, dtype=f32)[None, :] * inv[:, None]
    cos = _np.tile(_np.cos(ang), (4, 1)).astype(f32)
    sin = _np.tile(_np.concatenate([-_np.sin(ang), _np.sin(ang)]), (2, 1)).astype(f32)
    ind = _np.zeros((P, 2), f32)
    ind[0:HEAD, 0] = 1.0 / HEAD
    ind[HEAD:P, 1] = 1.0 / HEAD
    mask = _np.triu(_np.full((P, P), MASKED, f32), 1)

    arrays = {
        "x": a["x"].reshape(TT, P, D),
        "wt": _np.stack(tiles),
        "vec": vec,
        "gain2": _np.ascontiguousarray(_np.broadcast_to(a["ffn_norm"][0], (P, D))),
        "lams": _np.ascontiguousarray(_np.broadcast_to(lams, (P, 4 * HEAD))),
        "ident": _np.eye(P, dtype=f32),
        "mask": mask,
        "cos": cos,
        "sin": sin,
        "ind": ind,
    }
    nc = _bacc.Bacc("TRN2", target_bir_lowering=False, num_devices=1)
    args = [nc.dram_tensor(n, v.shape, _mybir.dt.from_np(v.dtype), kind="ExternalInput").ap() for n, v in arrays.items()]
    out = nc.dram_tensor("out", (TT, P, D), _mybir.dt.float32, kind="ExternalOutput").ap()
    build(nc, *args, out)
    r = _run(nc, [arrays], core_ids=[0])
    return r.results[0]["out"].reshape(1, SEQ, D)
```

```python
from contextlib import ExitStack

import concourse.bass as bass
from concourse import mybir

ALU = mybir.AluOpType
ACT = mybir.ActivationFunctionType
AX = mybir.AxisListType
F32 = mybir.dt.float32
F32R = mybir.dt.float32r
U32 = mybir.dt.uint32

P = 128
SEQ = 512
D = 1024
FFN = 2816
HEAD = 64
EPS = 1e-6
BLOCK = 256
TT = SEQ // P
KT = D // P
PAIRS = 8
MOBA_PAIRS = 4
FT = FFN // P
LAMBDA_INIT = 0.8 - 0.6 * 1.0
NEWTON = 3
NEWTON_OPS = 3 + 3 * NEWTON
RSQRT_MAGIC = 0x5F3759DF
MASKED = -(2.0 ** 127)

G_OUT = 3 * PAIRS
G_FFN = G_OUT + KT
G_DOWN = G_FFN + 2 * FT
TILES = G_DOWN + FT

assert SEQ // BLOCK == 2, "MoBA is causal attention for two blocks only"


def raw_slot(g):
    return g % 3 if g < G_OUT + 3 else g % 4


def raw_loads(g):
    if g < G_OUT + 3:
        return g // 3 + 1
    return 1 + (g - 27) // 4 if g % 4 == 3 else 10 + (g - 28) // 4


def build(nc, x, wt, vec, gain2, lams, ident_in, mask_in, cos_in, sin_in, out):
    with ExitStack() as ctx:
        cursor = [16512]

        def place(name, shape, dt, at=None):
            n = 4
            for s in shape[1:]:
                n *= s
            if at is None:
                at = cursor[0]
                cursor[0] += n
            return nc.alloc_sbuf_tensor_at(name, shape, dt, offset=at), at

        def sem(name):
            return ctx.enter_context(nc.semaphore(name))

        X, _ = place("residual", [P, TT, D], F32)
        RAW, _ = place("w_raw", [P, 4, D], F32)
        WH, at_wh = place("w_hi", [P, 4, D], F32R)
        WL, at_wl = place("w_lo", [P, 4, D], F32R)
        ident, _ = place("ident", [P, P], F32)
        identR, _ = place("ident_r", [P, P], F32R)
        maskR, _ = place("mask_r", [P, P], F32R)
        cosT, _ = place("cos", [P, SEQ], F32)
        sinT, _ = place("sin", [P, SEQ], F32)
        small, _ = place("small", [P, 208], F32)
        QG, at_tmp = place("q_gained", [P, SEQ], F32)
        QR, _ = place("q_rotated", [P, SEQ], F32)
        QS, _ = place("q_roped", [P, SEQ], F32)
        KG, _ = place("k_gained", [P, SEQ], F32)
        KR, _ = place("k_rotated", [P, SEQ], F32)
        KS, _ = place("k_roped", [P, SEQ], F32)
        VT, _ = place("v_by_dim", [P, SEQ], F32)
        SG, _ = place("silu_gate", [P, 2, SEQ], F32, at_tmp)
        AC, _ = place("gated", [P, 2, SEQ], F32, at_tmp + 4096)
        KB = 1024
        H1, r0 = place("h_parts", [P, KT, 2, SEQ], F32R)
        MIX, r1 = place("mixed_parts", [P, KT, 2, SEQ], F32R)
        HID, _ = place("hidden_parts", [P, FT, 2, SEQ], F32R, r0)
        r2 = r1 + 32 * KB
        VH, _ = place("v_hi", [P, 2, TT, P], F32R, r2)
        VL, _ = place("v_lo", [P, 2, TT, P], F32R, r2 + 4 * KB)
        QH, _ = place("q_hi", [P, SEQ], F32R, r2 + 8 * KB)
        QL, _ = place("q_lo", [P, SEQ], F32R, r2 + 10 * KB)
        KH, _ = place("k_hi", [P, SEQ], F32R, r2 + 12 * KB)
        KL, _ = place("k_lo", [P, SEQ], F32R, r2 + 14 * KB)
        SQQ, _ = place("q_squared", [P, SEQ], F32, r2 + 16 * KB)
        SQK, _ = place("k_squared", [P, SEQ], F32, r2 + 18 * KB)
        KBC, _ = place("k_rstd_spread", [P, TT, 2, HEAD], F32, r2 + 20 * KB)
        ON, _ = place("o_normed", [P, TT, P], F32, r2 + 22 * KB)
        LAM0, _ = place("lambda_in", [P, 4 * HEAD], F32, r2 + 20 * KB)
        MASK0, _ = place("mask_in", [P, P], F32, r2 + 22 * KB)
        HN2, _ = place("h2_normed", [P, TT, D], F32, r2)
        JUNK2, _ = place("squares2", [P, D], F32, r2 + 16 * KB)
        G2, _ = place("ffn_gain", [P, D], F32, r2 + 20 * KB)
        r3 = r2 + 24 * KB
        H2, _ = place("h2_parts", [P, KT, 2, SEQ], F32R, r3)
        PTH, _ = place("probsT_hi", [P, 2, TT, SEQ], F32R, r3)
        PTL, _ = place("probsT_lo", [P, 2, TT, SEQ], F32R, r3 + 16 * KB)
        HN, _ = place("h_normed", [P, TT, D], F32, r3)
        JUNK, _ = place("squares", [P, 2, D], F32, r3 + 16 * KB)
        PR0, _ = place("probs_0", [P, 2, SEQ], F32, at_wh + 3 * 4 * D)
        PR1, _ = place("probs_1", [P, 2, SEQ], F32, at_wl + 3 * 4 * D)
        PR = (PR0, PR1)

        VEC = small[:, 0:28]
        IND = small[:, 26:28]
        NA = small[:, 32:48]
        NT = small[:, 48:64]
        NY = small[:, 64:80]
        NZ = small[:, 80:96]
        RQ = small[:, 96:104]
        SUM = small[:, 104:112]
        RS = small[:, 112:120]
        MX = small[:, 120:128]
        NB = small[:, 128:136]
        SS = small[:, 136:140]
        SO = small[:, 140:144]
        LP = small[:, 144:148]
        LAM = small[:, 148:149]
        SUBG = small[:, 149:150]
        NL = small[:, 152:156]
        S2 = small[:, 156:160]
        NX = small[:, 160:164]

        ps = ctx.enter_context(nc.psum_tensor("ps", [P, 8, SEQ], F32))

        x_in = [sem(f"x_in{t}") for t in range(TT)]
        ident_in_s = sem("ident_in")
        small_in = sem("small_in")
        rope_in = sem("rope_in")
        misc_in = sem("misc_in")
        gain2_in = sem("gain2_in")
        raw_in = [sem(f"raw_in{s}") for s in range(4)]
        w_hi = sem("w_hi_ready")
        w_lo = sem("w_lo_ready")
        w_used = sem("w_used")
        x_sq = sem("x_squared")
        x_sq_dve = sem("x_squared_dve")
        newton = sem("newton_step")
        hn_act = sem("h_normed_by_act")
        s2_s = sem("residual_squared")
        hn = sem("h_normed_ready")
        x_turned = sem("x_turned")
        hh = sem("h_hi_ready")
        hl = sem("h_lo_ready")
        consts = sem("consts_ready")
        lam_dot = sem("lambda_dots")
        lam_exp = sem("lambda_exps")
        lam_s = sem("lambda_ready")
        pads = sem("v_pads_cleared")
        q_ev = sem("q_evacuated")
        k_ev = sem("k_evacuated")
        v_ev = sem("v_evacuated")
        q_rot = sem("q_rotated_in")
        k_rot = sem("k_rotated_in")
        q_pool = sem("q_rope_step")
        k_pool = sem("k_rope_step")
        qh_s, ql_s, kh_s, kl_s = sem("q_hi_ready"), sem("q_lo_ready"), sem("k_hi_ready"), sem("k_lo_ready")
        kn_s = sem("k_normed")
        ms_s = sem("mean_squares")
        rq_s = sem("q_scale_ready")
        kbc_s = sem("k_rstd_spread_ready")
        kb_s = sem("k_rstd_turned")
        v_turn = sem("v_turned")
        vh_s, vl_s = sem("v_hi_ready"), sem("v_lo_ready")
        sc_s = sem("scores_ready")
        mx_s = sem("max_found")
        nb_s = sem("bias_ready")
        ex_s = sem("exp_ready")
        rs_s = sem("sums_inverted")
        lr_s = sem("map1_scaled")
        pn_s = sem("probs_normed")
        pt_s = sem("probs_turned")
        ph_s, pl_s = sem("probsT_hi_ready"), sem("probsT_lo_ready")
        pv_s = sem("heads_out")
        o_sq = sem("o_squared")
        on_s = sem("o_normed_ready")
        o_turn = sem("o_turned")
        mh_s, ml_s = sem("mixed_hi_ready"), sem("mixed_lo_ready")
        wo_s = sem("out_rows")
        res = sem("residual_added")
        h2_turned = sem("h2_turned")
        h2h, h2l = sem("h2_hi_ready"), sem("h2_lo_ready")
        silu_s, gated_s = sem("silu_ready"), sem("gated_ready")
        ah_s, al_s = sem("hidden_hi_ready"), sem("hidden_lo_ready")
        y_done = sem("down_rows")
        y_add = sem("output_added")
        stored = sem("stored")

        def turned(t, qt, a):
            if t < MOBA_PAIRS:
                return 8 * t + 2 * qt + a + 1
            return 8 * MOBA_PAIRS + 4 * (t - MOBA_PAIRS) + qt + 1

        def raw_as(g):
            raw = RAW[:, raw_slot(g)]
            return raw.rearrange("p (k n) -> p k n", k=2) if 27 <= g < 31 else raw

        def used(g):
            return g + 1 if g < G_OUT else g + 1 - KT

        block = ctx.enter_context(nc.Block())

        @block.sync
        def _(sp):
            def load(g):
                if g >= 28:
                    sp.wait_ge(w_lo, g - 3)
                elif 3 <= g < 27:
                    sp.wait_ge(w_lo, g - 2)
                s = raw_slot(g)
                sp.dma_start(RAW[:, s], wt[g]).then_inc(raw_in[s], 16)

            def rotate(dst, src, evac, pool, done, p):
                sp.wait_ge(evac, 2 * p + 2)
                if p >= 1:
                    sp.wait_ge(pool, 3 * p)
                for b in range(4):
                    sp.dma_start(dst[32 * b:32 * b + 32], src[32 * (b ^ 1):32 * (b ^ 1) + 32]).then_inc(done, 16)

            for t in range(TT):
                sp.dma_start(X[:, t], x[t]).then_inc(x_in[t], 16)
                if t == 0:
                    sp.dma_start(ident[:], ident_in).then_inc(ident_in_s, 16)
                    sp.dma_start(small[:, 0:28], vec).then_inc(small_in, 16)
            load(0)
            sp.dma_start(MASK0[:], mask_in).then_inc(misc_in, 16)
            sp.dma_start(LAM0[:], lams).then_inc(misc_in, 16)
            load(1)
            sp.dma_start(cosT[:], cos_in).then_inc(rope_in, 16)
            sp.dma_start(sinT[:], sin_in).then_inc(rope_in, 16)
            load(2)
            for p in range(PAIRS):
                load(3 * p + 3)
                rotate(QR, QG, q_ev, q_pool, q_rot, p)
                load(3 * p + 4)
                rotate(KR, KG, k_ev, k_pool, k_rot, p)
                load(3 * p + 5)
            for g in range(27, 32):
                load(g)
            sp.wait_ge(o_turn, PAIRS - MOBA_PAIRS)
            sp.dma_start(G2[:], gain2).then_inc(gain2_in, 16)
            for g in range(32, TILES):
                load(g)
            for tt in range(TT):
                for half in range(2):
                    sp.wait_ge(y_add, 2 * tt + half + 1)
                    sp.dma_start(out[tt, :, half * SEQ:(half + 1) * SEQ],
                                 X[:, tt, half * SEQ:(half + 1) * SEQ]).then_inc(stored, 16)
            sp.wait_ge(stored, 16 * 2 * TT)

        @block.gpsimd
        def _(pool):
            def rope(p, G, R, S, ev, rot, step, hi, lo):
                pool.wait_ge(ev, 2 * p + 2)
                if p >= 1:
                    pool.wait_ge(hi, p)
                    pool.wait_ge(lo, p)
                nc.gpsimd.tensor_tensor(S[:], G[:], cosT[:], ALU.mult).then_inc(step, 1)
                pool.wait_ge(rot, 64 * (p + 1))
                nc.gpsimd.tensor_tensor(R[:], R[:], sinT[:], ALU.mult).then_inc(step, 1)
                pool.wait_ge(step, 3 * p + 2)
                nc.gpsimd.tensor_tensor(S[:], S[:], R[:], ALU.add).then_inc(step, 1)

            pool.wait_ge(rope_in, 32)
            for p in range(PAIRS):
                rope(p, QG, QR, QS, q_ev, q_rot, q_pool, qh_s, ql_s)
                rope(p, KG, KR, KS, k_ev, k_rot, k_pool, kh_s, kl_s)

        @block.scalar
        def _(act):
            def split_hi(g):
                act.wait_ge(raw_in[raw_slot(g)], 16 * raw_loads(g))
                if g < 27:
                    if g >= 3:
                        act.wait_ge(w_used, g - 2)
                    dst = WH[:, g % 3]
                elif g < 31:
                    act.wait_ge(w_used, G_OUT)
                    dst = H1[:, 2 * (g - 27):2 * (g - 27) + 2, 0]
                else:
                    if g == 31:
                        act.wait_ge(pt_s, turned(PAIRS - 1, TT - 1, 1))
                    else:
                        if g < G_FFN + 4:
                            act.wait_ge(wo_s, TT)
                        else:
                            act.wait_ge(w_used, used(g - 4))
                    dst = WH[:, g % 4]
                nc.scalar.activation(dst, raw_as(g), ACT.Copy).then_inc(w_hi, 1)

            def evacuate(p, j, bank, SQ, G, ev, col, evs):
                act.wait_ge(w_used, 3 * p + j + 1)
                if p >= 1:
                    act.wait_ge(ms_s, p)
                if p > MOBA_PAIRS + 1:
                    act.wait_ge(o_sq, p - MOBA_PAIRS - 1)
                nc.scalar.activation(SQ[:], ps[:, bank], ACT.Square).then_inc(ev, 1)
                if p >= 1:
                    act.wait_ge(evs, 3 * p)
                nc.scalar.activation(G[:], ps[:, bank], ACT.Copy, scale=VEC[:, col:col + 1]).then_inc(ev, 1)

            def q_evac(p):
                evacuate(p, 0, 0, SQQ, QG, q_ev, 8 + p, q_pool)

            def k_evac(p):
                evacuate(p, 1, 1, SQK, KG, k_ev, 16 + p, k_pool)

            def v_evac(p):
                act.wait_ge(w_used, 3 * p + 3)
                if p >= 1:
                    act.wait_ge(v_turn, p)
                nc.scalar.activation(VT[:], ps[:, 0], ACT.Copy).then_inc(v_ev, 1)

            def q_hi(p):
                act.wait_ge(q_pool, 3 * p + 3)
                if p >= 1:
                    act.wait_ge(sc_s, 8 * p)
                nc.scalar.activation(QH[:], QS[:], ACT.Copy).then_inc(qh_s, 1)

            def k_hi(p):
                act.wait_ge(kn_s, p + 1)
                if p >= 1:
                    act.wait_ge(sc_s, 8 * p)
                nc.scalar.activation(KH[:], KS[:], ACT.Copy).then_inc(kh_s, 1)

            def v_hi(t):
                act.wait_ge(v_turn, t + 1)
                act.wait_ge(pads, 1)
                if t >= 1:
                    act.wait_ge(pv_s, t)
                turned_v = ps[:, 7].rearrange("p (t d) -> p t d", t=TT)
                if t < MOBA_PAIRS:
                    nc.scalar.activation(VH[:, 0, :, 0:HEAD], turned_v[:, :, 0:HEAD], ACT.Copy)
                    nc.scalar.activation(VH[:, 1, :, HEAD:P], turned_v[:, :, HEAD:P], ACT.Copy).then_inc(vh_s, 1)
                else:
                    nc.scalar.activation(VH[:, 0], turned_v, ACT.Copy).then_inc(vh_s, 1)

            def exps(t, qt):
                W = (qt + 1) * P
                for a in range(2):
                    i = 2 * qt + a
                    act.wait_ge(nb_s, 8 * t + i + 1)
                    if t >= 1 or qt >= 2:
                        before = (t, qt - 2) if qt >= 2 else (t - 1, qt + 2)
                        act.wait_ge(pt_s, turned(before[0], before[1], a if before[0] < MOBA_PAIRS else 1))
                    nc.scalar.activation(PR[qt % 2][:, a, 0:W], ps[:, 2 + a, 0:W], ACT.Exp, bias=NB[:, i:i + 1],
                                         scale=RQ[:, i:i + 1], accum_out=SUM[:, i:i + 1]).then_inc(ex_s, 1)

            def maps(t):
                return range(2) if t < MOBA_PAIRS else range(1)

            def pt_hi(t, qt):
                for a in maps(t):
                    act.wait_ge(pt_s, turned(t, qt, a))
                    if t >= 1:
                        act.wait_ge(pv_s, t)
                    bank = 4 + (a if t < MOBA_PAIRS else qt % 2)
                    nc.scalar.activation(PTH[:, a, 0:qt + 1, qt * P:(qt + 1) * P],
                                         ps[:, bank, 0:(qt + 1) * P].rearrange("p (k q) -> p k q", q=P),
                                         ACT.Copy).then_inc(ph_s, 1)

            def o_squares(t):
                act.wait_ge(pv_s, t + 1)
                act.wait_ge(ms_s, min(t + 2, PAIRS))
                for qt in range(TT):
                    qs = slice(qt * P, (qt + 1) * P)
                    ins = nc.scalar.activation(SQQ[:, qs], ps[:, 6, qs], ACT.Square, accum_out=SO[:, qt:qt + 1])
                ins.then_inc(o_sq, 1)

            def mix_hi(t):
                if t < MOBA_PAIRS:
                    act.wait_ge(pv_s, t + 1)
                    nc.scalar.activation(MIX[:, t, 0], ps[:, 6], ACT.Copy).then_inc(mh_s, 1)
                else:
                    act.wait_ge(o_turn, t - MOBA_PAIRS + 1)
                    nc.scalar.activation(MIX[:, t, 0], ps[:, 6], ACT.Copy, scale=SUBG).then_inc(mh_s, 1)

            for n, t in enumerate((0, 2)):
                act.wait_ge(x_in[t], 16)
                if n == 1:
                    act.wait_ge(x_sq, 1)
                nc.scalar.activation(JUNK[:, 0], X[:, t], ACT.Square, accum_out=SS[:, t:t + 1]).then_inc(x_sq, 1)
            split_hi(0)
            act.wait_ge(hn, 1)
            nc.scalar.activation(HN[:, 0], X[:, 0], ACT.Copy, scale=NX[:, 0:1]).then_inc(hn_act, 1)
            act.wait_ge(ident_in_s, 16)
            nc.scalar.activation(identR[:], ident[:], ACT.Copy).then_inc(consts, 1)
            act.wait_ge(small_in, 16)
            for k in range(KT):
                act.wait_ge(x_turned, k + 1)
                nc.scalar.activation(H1[:, k, 0], ps[:, k], ACT.Copy, scale=VEC[:, k:k + 1]).then_inc(hh, 1)
            split_hi(1)
            act.wait_ge(misc_in, 32)
            nc.scalar.activation(maskR[:], MASK0[:], ACT.Copy).then_inc(consts, 1)
            act.wait_ge(lam_dot, 2)
            nc.scalar.activation(LP[:, 2:4], LP[:, 0:2], ACT.Exp).then_inc(lam_exp, 1)
            split_hi(2)
            q_evac(0)
            split_hi(3)
            k_evac(0)
            q_hi(0)
            v_evac(0)
            k_hi(0)
            split_hi(4)
            for t in range(PAIRS):
                p = t + 1
                more = p < PAIRS
                v_hi(t)
                exps(t, 0)
                if t > MOBA_PAIRS:
                    o_squares(t - 1)
                exps(t, 1)
                split_hi(3 * p + 2)
                exps(t, 2)
                if more:
                    q_evac(p)
                pt_hi(t, 0)
                exps(t, 3)
                pt_hi(t, 1)
                split_hi(3 * p + 3)
                if t > MOBA_PAIRS:
                    mix_hi(t - 1)
                pt_hi(t, 2)
                if more:
                    k_evac(p)
                pt_hi(t, 3)
                if more:
                    q_hi(p)
                    v_evac(p)
                    k_hi(p)
                if t < MOBA_PAIRS:
                    mix_hi(t)
                split_hi(3 * p + 4)
            for g in range(3 * PAIRS + 5, G_FFN):
                split_hi(g)
            o_squares(PAIRS - 1)
            mix_hi(PAIRS - 1)

            def h2_hi(tt):
                act.wait_ge(h2_turned, tt + 1)
                b = 2 * (tt % 2)
                nc.scalar.activation(H2[:, :, 0, tt * P:(tt + 1) * P],
                                     ps[:, b:b + 2].rearrange("p b (k q) -> p (b k) q", q=P),
                                     ACT.Copy).then_inc(h2h, 1)

            split_hi(G_FFN)
            split_hi(G_FFN + 1)
            for tt in range(TT):
                act.wait_ge(res, TT + tt + 1)
                if tt >= 1:
                    act.wait_ge(s2_s, tt)
                nc.scalar.activation(JUNK2[:], X[:, tt], ACT.Square, accum_out=S2[:, tt:tt + 1]).then_inc(s2_s, 1)
                if tt >= 1:
                    h2_hi(tt - 1)
                if tt < 2:
                    split_hi(G_FFN + 2 + tt)
            h2_hi(TT - 1)

            def silu(f):
                act.wait_ge(w_used, used(G_FFN + 2 * f))
                if f >= 2:
                    act.wait_ge(gated_s, f - 1)
                nc.scalar.activation(SG[:, f % 2], ps[:, 4 + 2 * (f % 2)], ACT.Silu).then_inc(silu_s, 1)

            def hidden_hi(f):
                act.wait_ge(gated_s, f + 1)
                nc.scalar.activation(HID[:, f, 0], AC[:, f % 2], ACT.Copy).then_inc(ah_s, 1)

            for f in range(FT):
                silu(f)
                g = G_FFN + 2 * f + 4
                if g < TILES:
                    split_hi(g)
                hidden_hi(f)
                if g + 1 < TILES:
                    split_hi(g + 1)
            for g in range(G_DOWN + 4, TILES):
                split_hi(g)

        @block.vector
        def _(dve):
            steps = [0]

            def step(ins):
                steps[0] += 1
                ins.then_inc(newton, 1)
                dve.wait_ge(newton, steps[0])

            def rsqrt(src, n, scale, at=0):
                a, h, y, z = (v[:, 0:n] for v in (NA, NT, NY, NZ))
                step(nc.vector.tensor_scalar(a, src, scale, EPS, ALU.mult, ALU.add))
                step(nc.vector.tensor_scalar(h.bitcast(U32), a.bitcast(U32), 1, None, ALU.logical_shift_right))
                step(nc.vector.tensor_scalar(y.bitcast(U32), h.bitcast(U32), -1.0, float(RSQRT_MAGIC),
                                             ALU.mult, ALU.add))
                for _ in range(NEWTON):
                    step(nc.vector.tensor_tensor(z, y, y, ALU.mult))
                    step(nc.vector.scalar_tensor_tensor(out=z, in0=z, scalar=-0.5, in1=a, op0=ALU.mult, op1=ALU.mult))
                    step(nc.vector.scalar_tensor_tensor(out=y, in0=z, scalar=1.5, in1=y, op0=ALU.add, op1=ALU.mult))
                return y

            def split_lo(g):
                dve.wait_ge(w_hi, g + 1)
                if g < 27:
                    hi, lo = WH[:, g % 3], WL[:, g % 3]
                elif g < 31:
                    hi, lo = (H1[:, 2 * (g - 27):2 * (g - 27) + 2, i] for i in range(2))
                else:
                    hi, lo = WH[:, g % 4], WL[:, g % 4]
                nc.vector.tensor_tensor(lo, raw_as(g), hi.bitcast(F32), ALU.subtract).then_inc(w_lo, 1)

            def q_lo(p):
                dve.wait_ge(qh_s, p + 1)
                nc.vector.tensor_tensor(QL[:], QS[:], QH[:].bitcast(F32), ALU.subtract).then_inc(ql_s, 1)

            def scales(p):
                dve.wait_ge(ms_s, p + 1)
                y = rsqrt(ps[:, 7, 0:16], 16, 1.0)
                if p >= 1:
                    dve.wait_ge(ex_s, 8 * p)
                nc.vector.tensor_scalar(RQ, y[:, 0:8], HEAD ** -0.5, None, ALU.mult).then_inc(rq_s, 1)
                if p >= 1:
                    dve.wait_ge(kb_s, p)
                nc.vector.tensor_copy(KBC[:].rearrange("p t a e -> p (t a) e"),
                                      y[:, 8:16].unsqueeze(2).broadcast_to([P, 8, HEAD])).then_inc(kbc_s, 1)

            def k_norm(p):
                dve.wait_ge(kb_s, p + 1)
                dve.wait_ge(k_pool, 3 * p + 3)
                nc.vector.tensor_tensor(KS[:], KS[:], ps[:, 7], ALU.mult).then_inc(kn_s, 1)
                dve.wait_ge(kh_s, p + 1)
                nc.vector.tensor_tensor(KL[:], KS[:], KH[:].bitcast(F32), ALU.subtract).then_inc(kl_s, 1)

            def v_lo(t):
                dve.wait_ge(vh_s, t + 1)
                turned_v = ps[:, 7].rearrange("p (t d) -> p t d", t=TT)
                if t < MOBA_PAIRS:
                    nc.vector.tensor_tensor(VL[:, 0, :, 0:HEAD], turned_v[:, :, 0:HEAD],
                                            VH[:, 0, :, 0:HEAD].bitcast(F32), ALU.subtract)
                    nc.vector.tensor_tensor(VL[:, 1, :, HEAD:P], turned_v[:, :, HEAD:P],
                                            VH[:, 1, :, HEAD:P].bitcast(F32), ALU.subtract).then_inc(vl_s, 1)
                else:
                    nc.vector.tensor_tensor(VL[:, 0], turned_v, VH[:, 0].bitcast(F32), ALU.subtract).then_inc(vl_s, 1)

            def maxima(t, qt):
                W = (qt + 1) * P
                for a in range(2):
                    i = 2 * qt + a
                    dve.wait_ge(sc_s, 8 * t + i + 1)
                    nc.vector.tensor_reduce(MX[:, i:i + 1], ps[:, 2 + a, 0:W], AX.X, ALU.max).then_inc(mx_s, 1)
                for a in range(2):
                    i = 2 * qt + a
                    dve.wait_ge(mx_s, 8 * t + i + 1)
                    dve.wait_ge(rq_s, t + 1)
                    nc.vector.scalar_tensor_tensor(out=NB[:, i:i + 1], in0=MX[:, i:i + 1], scalar=-1.0,
                                                   in1=RQ[:, i:i + 1], op0=ALU.mult, op1=ALU.mult).then_inc(nb_s, 1)

            def norm(t, qt):
                W = (qt + 1) * P
                i = 2 * qt
                p0, p1 = PR[qt % 2][:, 0, 0:W], PR[qt % 2][:, 1, 0:W]
                dve.wait_ge(ex_s, 8 * t + i + 2)
                nc.vector.reciprocal(RS[:, i:i + 2], SUM[:, i:i + 2]).then_inc(rs_s, 1)
                dve.wait_ge(rs_s, 4 * t + qt + 1)
                if t < MOBA_PAIRS:
                    nc.vector.tensor_scalar(p0, p0, RS[:, i:i + 1], None, ALU.mult).then_inc(pn_s, 1)
                    nc.vector.tensor_scalar(p1, p1, RS[:, i + 1:i + 2], None, ALU.mult).then_inc(pn_s, 1)
                else:
                    n = 2 * (4 * (t - MOBA_PAIRS) + qt)
                    nc.vector.tensor_tensor(NL[:, qt:qt + 1], RS[:, i + 1:i + 2], LAM, ALU.mult).then_inc(lr_s, 1)
                    dve.wait_ge(lr_s, n + 1)
                    nc.vector.tensor_scalar(p1, p1, NL[:, qt:qt + 1], None, ALU.mult).then_inc(lr_s, 1)
                    dve.wait_ge(lr_s, n + 2)
                    nc.vector.scalar_tensor_tensor(out=p0, in0=p0, scalar=RS[:, i:i + 1], in1=p1,
                                                   op0=ALU.mult, op1=ALU.subtract).then_inc(pn_s, 1)

            def pt_lo(t, qt):
                for a in (range(2) if t < MOBA_PAIRS else range(1)):
                    dve.wait_ge(ph_s, turned(t, qt, a))
                    bank = 4 + (a if t < MOBA_PAIRS else qt % 2)
                    at = (slice(None), a, slice(0, qt + 1), slice(qt * P, (qt + 1) * P))
                    nc.vector.tensor_tensor(PTL[at], ps[:, bank, 0:(qt + 1) * P].rearrange("p (k q) -> p k q", q=P),
                                            PTH[at].bitcast(F32), ALU.subtract).then_inc(pl_s, 1)

            def o_norm(t):
                dve.wait_ge(o_sq, t - MOBA_PAIRS + 1)
                y = rsqrt(SO, 4, 1.0 / P)
                for qt in range(TT):
                    ins = nc.vector.tensor_scalar(ON[:, qt], ps[:, 6, qt * P:(qt + 1) * P], y[:, qt:qt + 1], None,
                                                  ALU.mult)
                ins.then_inc(on_s, 1)

            def mix_lo(t):
                dve.wait_ge(mh_s, t + 1)
                if t < MOBA_PAIRS:
                    nc.vector.tensor_tensor(MIX[:, t, 1], ps[:, 6], MIX[:, t, 0].bitcast(F32), ALU.subtract).then_inc(ml_s, 1)
                else:
                    nc.vector.scalar_tensor_tensor(out=MIX[:, t, 1], in0=ps[:, 6], scalar=SUBG, in1=MIX[:, t, 0].bitcast(F32),
                                                   op0=ALU.mult, op1=ALU.subtract).then_inc(ml_s, 1)

            for n, t in enumerate((1, 3)):
                dve.wait_ge(x_in[t], 16)
                if n == 1:
                    dve.wait_ge(x_sq_dve, 1)
                nc.vector.scalar_tensor_tensor(out=JUNK[:, 1], in0=X[:, t], scalar=1.0, in1=X[:, t], op0=ALU.mult,
                                               op1=ALU.mult, accum_out=SS[:, t:t + 1]).then_inc(x_sq_dve, 1)
            dve.wait_ge(x_sq, 2)
            dve.wait_ge(x_sq_dve, 2)
            y = rsqrt(SS, TT, 1.0 / D)
            nc.vector.tensor_copy(NX, y).then_inc(hn, 1)
            for t in range(1, TT):
                nc.vector.tensor_scalar(HN[:, t], X[:, t], y[:, t:t + 1], None, ALU.mult).then_inc(hn, 1)
            split_lo(0)
            dve.wait_ge(small_in, 16)
            for k in range(KT):
                dve.wait_ge(hh, k + 1)
                nc.vector.scalar_tensor_tensor(out=H1[:, k, 1], in0=ps[:, k], scalar=VEC[:, k:k + 1],
                                               in1=H1[:, k, 0].bitcast(F32), op0=ALU.mult,
                                               op1=ALU.subtract).then_inc(hl, 1)
            split_lo(1)
            dve.wait_ge(misc_in, 32)
            for j in range(2):
                step(nc.vector.tensor_tensor(LAM0[:, 2 * j * HEAD:(2 * j + 1) * HEAD],
                                             LAM0[:, 2 * j * HEAD:(2 * j + 1) * HEAD],
                                             LAM0[:, (2 * j + 1) * HEAD:(2 * j + 2) * HEAD], ALU.mult))
                nc.vector.tensor_reduce(LP[:, j:j + 1], LAM0[:, 2 * j * HEAD:(2 * j + 1) * HEAD], AX.X,
                                        ALU.add).then_inc(lam_dot, 1)
            nc.vector.memset(VH[:, 0, :, HEAD:P].bitcast(F32), 0.0)
            nc.vector.memset(VH[:, 1, :, 0:HEAD].bitcast(F32), 0.0)
            nc.vector.memset(VL[:, 0, :, HEAD:P].bitcast(F32), 0.0)
            nc.vector.memset(VL[:, 1, :, 0:HEAD].bitcast(F32), 0.0).then_inc(pads, 1)
            nc.vector.tensor_scalar(SUBG, VEC[:, 24:25], 1.0 - LAMBDA_INIT, None, ALU.mult)
            dve.wait_ge(lam_exp, 1)
            step(nc.vector.tensor_tensor(LAM, LP[:, 2:3], LP[:, 3:4], ALU.subtract))
            nc.vector.tensor_scalar(LAM, LAM, LAMBDA_INIT, None, ALU.add).then_inc(lam_s, 1)
            split_lo(2)
            split_lo(3)
            scales(0)
            q_lo(0)
            k_norm(0)
            split_lo(4)
            dve.wait_ge(lam_s, 1)
            for t in range(PAIRS):
                p = t + 1
                more = p < PAIRS
                v_lo(t)
                maxima(t, 0)
                maxima(t, 1)
                norm(t, 0)
                split_lo(3 * p + 2)
                maxima(t, 2)
                norm(t, 1)
                if t > MOBA_PAIRS:
                    o_norm(t - 1)
                pt_lo(t, 0)
                maxima(t, 3)
                norm(t, 2)
                pt_lo(t, 1)
                split_lo(3 * p + 3)
                norm(t, 3)
                if t > MOBA_PAIRS:
                    mix_lo(t - 1)
                pt_lo(t, 2)
                pt_lo(t, 3)
                if more:
                    q_lo(p)
                    scales(p)
                    k_norm(p)
                if t < MOBA_PAIRS:
                    mix_lo(t)
                split_lo(3 * p + 4)
            for g in range(3 * PAIRS + 5, G_FFN):
                split_lo(g)
            o_norm(PAIRS - 1)
            mix_lo(PAIRS - 1)

            def add_residual(half, tt):
                dve.wait_ge(wo_s, TT * half + tt + 1)
                at = (slice(None), tt, slice(half * SEQ, (half + 1) * SEQ))
                nc.vector.tensor_tensor(X[at], ps[:, 4 * half + tt], X[at], ALU.add).then_inc(res, 1)

            def h2_lo(tt):
                dve.wait_ge(h2h, tt + 1)
                b = 2 * (tt % 2)
                qs = slice(tt * P, (tt + 1) * P)
                nc.vector.tensor_tensor(H2[:, :, 1, qs], ps[:, b:b + 2].rearrange("p b (k q) -> p (b k) q", q=P),
                                        H2[:, :, 0, qs].bitcast(F32), ALU.subtract).then_inc(h2l, 1)

            for tt in range(TT):
                add_residual(0, tt)
            split_lo(G_FFN)
            split_lo(G_FFN + 1)
            dve.wait_ge(gain2_in, 16)
            for tt in range(TT):
                add_residual(1, tt)
                dve.wait_ge(s2_s, tt + 1)
                y = rsqrt(S2[:, tt:tt + 1], 1, 1.0 / D)
                nc.vector.scalar_tensor_tensor(out=HN2[:, tt], in0=X[:, tt], scalar=y, in1=G2[:], op0=ALU.mult,
                                               op1=ALU.mult).then_inc(hn, 1)
                if tt >= 1:
                    h2_lo(tt - 1)
                if tt < 2:
                    split_lo(G_FFN + 2 + tt)
            h2_lo(TT - 1)
            for f in range(FT):
                dve.wait_ge(silu_s, f + 1)
                dve.wait_ge(w_used, used(G_FFN + 2 * f + 1))
                if f >= 2:
                    dve.wait_ge(ah_s, f - 1)
                    dve.wait_ge(al_s, f - 1)
                nc.vector.tensor_tensor(AC[:, f % 2], ps[:, 5 + 2 * (f % 2)], SG[:, f % 2], ALU.mult).then_inc(gated_s, 1)
                g = G_FFN + 2 * f + 4
                if g < TILES:
                    split_lo(g)
                dve.wait_ge(ah_s, f + 1)
                nc.vector.tensor_tensor(HID[:, f, 1], AC[:, f % 2], HID[:, f, 0].bitcast(F32), ALU.subtract).then_inc(al_s, 1)
                if g + 1 < TILES:
                    split_lo(g + 1)
            for g in range(G_DOWN + 4, TILES):
                split_lo(g)
            for tt in range(TT):
                for half in range(2):
                    dve.wait_ge(y_done, 2 * tt + half + 1)
                    at = (slice(None), tt, slice(half * SEQ, (half + 1) * SEQ))
                    nc.vector.tensor_tensor(X[at], ps[:, 2 * tt + half], X[at], ALU.add).then_inc(y_add, 1)

        @block.tensor
        def _(pe):
            def product(dst, lh, ll, rh, rl, start, stop):
                nc.tensor.matmul(dst, lh, rh, start=start, stop=False, skip_group_check=True)
                nc.tensor.matmul(dst, lh, rl, start=False, stop=False, skip_group_check=True)
                return nc.tensor.matmul(dst, ll, rh, start=False, stop=stop, skip_group_check=True)

            def project(p, n):
                j, k = divmod(n, KT)
                g = 3 * p + j
                if k == 0:
                    pe.wait_ge(w_hi, g + 1)
                    pe.wait_ge(w_lo, g + 1)
                    if j == 0 and p >= 1:
                        pe.wait_ge(v_ev, p)
                    if j == 1 and p >= 1:
                        pe.wait_ge(k_ev, 2 * p)
                    if j == 2:
                        pe.wait_ge(q_ev, 2 * p + 2)
                if g == 0:
                    pe.wait_ge(hh, k + 1)
                    pe.wait_ge(hl, k + 1)
                w = slice(k * P, (k + 1) * P)
                ins = product(ps[:, j % 2], WH[:, j, w], WL[:, j, w], H1[:, k, 0], H1[:, k, 1], k == 0, k == KT - 1)
                if k == KT - 1:
                    ins.then_inc(w_used, 1)

            def mean_squares(p):
                pe.wait_ge(k_ev, 2 * p + 1)
                if p >= 1:
                    pe.wait_ge(vl_s, p)
                for j, SQ in enumerate((SQQ, SQK)):
                    for tt in range(TT):
                        c = 2 * (TT * j + tt)
                        ins = nc.tensor.matmul(ps[:, 7, c:c + 2], SQ[:, tt * P:(tt + 1) * P], IND, start=True, stop=True,
                                               skip_group_check=True)
                ins.then_inc(ms_s, 1)

            def spread_k(p):
                pe.wait_ge(kbc_s, p + 1)
                for tt in range(TT):
                    ins = nc.tensor.transpose(ps[:, 7, tt * P:(tt + 1) * P],
                                              KBC[:, tt].rearrange("p a e -> p (a e)"), ident[:])
                ins.then_inc(kb_s, 1)

            def turn_v(t):
                pe.wait_ge(v_ev, t + 1)
                pe.wait_ge(kn_s, t + 1)
                for tt in range(TT):
                    ins = nc.tensor.transpose(ps[:, 7, tt * P:(tt + 1) * P], VT[:, tt * P:(tt + 1) * P], ident[:])
                ins.then_inc(v_turn, 1)

            def scores(t, qt):
                W = (qt + 1) * P
                qs = slice(qt * P, W)
                if qt == 0:
                    for s in (qh_s, ql_s, kh_s, kl_s):
                        pe.wait_ge(s, t + 1)
                if t >= 1 or qt >= 1:
                    pe.wait_ge(ex_s, 8 * t + 2 * qt)
                rows = (slice(0, HEAD), slice(HEAD, P))
                for left, right, first in ((QH, KH, True), (QH, KL, False), (QL, KH, False)):
                    for a in range(2):
                        nc.tensor.matmul(ps[:, 2 + a, 0:W], left[rows[a], qs], right[rows[a], 0:W], start=first,
                                         stop=False, skip_group_check=True)
                pe.wait_ge(consts, 2)
                for a in range(2):
                    nc.tensor.matmul(ps[:, 2 + a, qs], identR[:], maskR[:], start=False, stop=True,
                                     skip_group_check=True).then_inc(sc_s, 1)

            def turn_p(t, qt):
                for a in (range(2) if t < MOBA_PAIRS else range(1)):
                    n = turned(t, qt, a)
                    pe.wait_ge(pn_s, n)
                    if n > 2:
                        pe.wait_ge(pl_s, n - 2)
                    bank = 4 + (a if t < MOBA_PAIRS else qt % 2)
                    for kt in range(qt + 1):
                        ins = nc.tensor.transpose(ps[:, bank, kt * P:(kt + 1) * P],
                                                  PR[qt % 2][:, a, kt * P:(kt + 1) * P], ident[:])
                    ins.then_inc(pt_s, 1)

            def heads_out(t, part):
                if part == 0:
                    pe.wait_ge(pl_s, turned(t, TT - 1, 1))
                    pe.wait_ge(vh_s, t + 1)
                    pe.wait_ge(vl_s, t + 1)
                    if t >= 1:
                        pe.wait_ge(ml_s, t)
                if t < MOBA_PAIRS:
                    for kt in range(TT):
                        ins = product(ps[:, 6, kt * P:SEQ], VH[:, part, kt], VL[:, part, kt],
                                      PTH[:, part, kt, kt * P:SEQ], PTL[:, part, kt, kt * P:SEQ],
                                      part == 0 and kt == 0, part == 1 and kt == TT - 1)
                else:
                    for qt in ((0, 1, 2), (3,))[part]:
                        for kt in range(qt + 1):
                            qs = slice(qt * P, (qt + 1) * P)
                            ins = product(ps[:, 6, qs], PTH[:, 0, kt, qs], PTL[:, 0, kt, qs], VH[:, 0, kt], VL[:, 0, kt],
                                          kt == 0, kt == qt)
                if part == 1:
                    ins.then_inc(pv_s, 1)

            def turn_o(t):
                pe.wait_ge(on_s, t - MOBA_PAIRS + 1)
                for qt in range(TT):
                    ins = nc.tensor.transpose(ps[:, 6, qt * P:(qt + 1) * P], ON[:, qt], ident[:])
                ins.then_inc(o_turn, 1)

            def w_out(half, tt, k):
                if half == 1:
                    g, wh, wl = G_OUT + 3 + k // 2, H1[:, k, 0], H1[:, k, 1]
                else:
                    cs = slice((k % 2) * SEQ, (k % 2 + 1) * SEQ)
                    g = G_OUT + (k // 2 if k < 6 else 7)
                    wh, wl = WH[:, k // 2, cs], WL[:, k // 2, cs]
                pe.wait_ge(w_lo, g + 1)
                pe.wait_ge(ml_s, k + 1)
                qs = slice(tt * P, (tt + 1) * P)
                ins = product(ps[:, 4 * half + tt], MIX[:, k, 0, qs], MIX[:, k, 1, qs], wh, wl, k == 0, k == KT - 1)
                if k == KT - 1:
                    ins.then_inc(wo_s, 1)

            pe.wait_ge(ident_in_s, 16)
            for n in range(13):
                nc.tensor.matmul(ps[:, 0, 0:P], ident[:], ident[:], start=True, stop=True)
            for n, tt in enumerate((1, 2, 0, 3)):
                if tt == 0:
                    pe.wait_ge(hn_act, 1)
                else:
                    pe.wait_ge(hn, tt + 1)
                for k in range(KT):
                    ins = nc.tensor.transpose(ps[:, k, tt * P:(tt + 1) * P], HN[:, tt, k * P:(k + 1) * P], ident[:])
                    if n == TT - 1:
                        ins.then_inc(x_turned, 1)
            for n in range(18):
                project(0, n)
            pe.wait_ge(hl, KT)
            mean_squares(0)
            for n in range(18, 24):
                project(0, n)
            for t in range(PAIRS):
                p = t + 1
                done = [0]

                def fill(n):
                    for _ in range(n):
                        m = done[0]
                        done[0] += 1
                        if p < PAIRS:
                            project(p, m)
                        elif m % 2 == 1:
                            if m == 1:
                                pe.wait_ge(v_ev, PAIRS)
                                pe.wait_ge(k_ev, 2 * PAIRS)
                            w_out(0, (m // 2) % 2, m // 4)

                fill(2)
                if t == 0:
                    spread_k(0)
                    fill(2)
                turn_v(t)
                fill(1)
                scores(t, 0)
                fill(3)
                scores(t, 1)
                fill(3 if t else 1)
                scores(t, 2)
                fill(2)
                turn_p(t, 0)
                fill(1)
                scores(t, 3)
                fill(2)
                turn_p(t, 1)
                if t > MOBA_PAIRS:
                    turn_o(t - 1)
                fill(2)
                turn_p(t, 2)
                fill(2)
                if p < PAIRS:
                    mean_squares(p)
                turn_p(t, 3)
                fill(3)
                heads_out(t, 0)
                fill(2)
                if p < PAIRS:
                    spread_k(p)
                fill(1)
                heads_out(t, 1)
            for tt in (2, 3):
                for k in range(6):
                    w_out(0, tt, k)
            turn_o(PAIRS - 1)
            for k in (6, 7):
                for tt in range(TT):
                    w_out(0, tt, k)

            def turn_h2(tt):
                pe.wait_ge(hn, TT + tt + 1)
                if tt >= 2:
                    pe.wait_ge(h2l, tt - 1)
                for k in range(KT):
                    b = 2 * (tt % 2) + k // 4
                    ins = nc.tensor.transpose(ps[:, b, (k % 4) * P:(k % 4 + 1) * P], HN2[:, tt, k * P:(k + 1) * P],
                                              ident[:])
                ins.then_inc(h2_turned, 1)

            for tt in range(TT):
                for k in range(KT):
                    w_out(1, tt, k)
                if tt >= 1 and tt < 3:
                    turn_h2(tt - 1)

            def hidden(f, j, cols):
                g = G_FFN + 2 * f + j
                pe.wait_ge(w_lo, g + 1)
                if f >= 2:
                    pe.wait_ge((silu_s, gated_s)[j], f - 1)
                for k in range(KT):
                    w = slice(k * P, (k + 1) * P)
                    ins = product(ps[:, 4 + 2 * (f % 2) + j, cols], WH[:, g % 4, w], WL[:, g % 4, w],
                                  H2[:, k, 0, cols], H2[:, k, 1, cols], k == 0, k == KT - 1)
                if cols.stop == SEQ:
                    ins.then_inc(w_used, 1)

            for n, (f, j) in enumerate(((0, 0), (0, 1), (1, 0), (1, 1))):
                pe.wait_ge(h2l, 2)
                pe.wait_ge(res, TT + n + 1)
                hidden(f, j, slice(0, SEQ // 2))
                if n == 0:
                    turn_h2(2)
                if n == 2:
                    turn_h2(3)
            pe.wait_ge(h2l, TT)
            for f, j in ((0, 0), (0, 1), (1, 0), (1, 1)):
                hidden(f, j, slice(SEQ // 2, SEQ))
            for f in range(2, FT):
                hidden(f, 0, slice(0, SEQ))
                hidden(f, 1, slice(0, SEQ))

            def down(f, tt, half):
                s = (G_DOWN + f) % 4
                qs, cs = slice(tt * P, (tt + 1) * P), slice(half * SEQ, (half + 1) * SEQ)
                return product(ps[:, 2 * tt + half], HID[:, f, 0, qs], HID[:, f, 1, qs], WH[:, s, cs], WL[:, s, cs],
                               f == 0, f == FT - 1)

            TAIL = 3
            for f in range(FT - TAIL):
                pe.wait_ge(w_lo, G_DOWN + f + 1)
                pe.wait_ge(al_s, f + 1)
                for tt in range(TT):
                    if f == 0 and tt == 2:
                        pe.wait_ge(gated_s, FT)
                    for half in range(2):
                        ins = down(f, tt, half)
                ins.then_inc(w_used, 1)
            pe.wait_ge(w_lo, TILES)
            pe.wait_ge(al_s, FT)
            for tt in range(TT):
                for half in range(2):
                    for f in range(FT - TAIL, FT):
                        ins = down(f, tt, half)
                    ins.then_inc(y_done, 1)


def kernel(**inputs):
    import numpy as _np
    import concourse.bacc as _bacc
    from concourse import mybir as _mybir
    from concourse.bass_utils import run_bass_kernel_spmd as _run

    a = {k: _np.ascontiguousarray(v) for k, v in inputs.items()}
    f32 = _np.float32

    def columns(w, c):
        return w[:, c:c + P].reshape(KT, P, P).transpose(1, 0, 2).reshape(P, D)

    w_in = a["w_in"][0]
    tiles = []
    for p in range(PAIRS):
        base, n = (0, p) if p < MOBA_PAIRS else (3 * MOBA_PAIRS * P, p - MOBA_PAIRS)
        for j in range(3):
            tiles.append(columns(w_in, base + (j * MOBA_PAIRS + n) * P))
    w_out = a["w_out"][0].reshape(KT // 2, 2, P, 2, SEQ).transpose(3, 0, 2, 1, 4).reshape(2, KT // 2, P, D)
    tiles += [w_out[0, 0], w_out[0, 1], w_out[0, 2], *w_out[1], w_out[0, 3]]
    for f in range(FT):
        tiles.append(columns(a["w_gate"][0], f * P))
        tiles.append(columns(a["w_up"][0], f * P))
    for f in range(FT):
        tiles.append(a["w_down"][0][f * P:(f + 1) * P])

    vec = _np.zeros((P, 28), f32)
    vec[:, 0:8] = a["attn_norm"][0].reshape(KT, P).T
    for p in range(PAIRS):
        kind = "moba" if p < MOBA_PAIRS else "diff"
        vec[:, 8 + p] = _np.tile(a[kind + "_q_norm"][0], 2)
        vec[:, 16 + p] = _np.tile(a[kind + "_k_norm"][0], 2)
    vec[:, 24] = a["diff_subln"][0]
    lams = _np.concatenate([a[n][0] for n in ("lambda_q1", "lambda_k1", "lambda_q2", "lambda_k2")])

    inv = (1.0 / (f32(10000.0) ** (_np.arange(0, HEAD, 2, dtype=f32) / f32(HEAD)))).astype(f32)
    ang = _np.arange(SEQ, dtype=f32)[None, :] * inv[:, None]
    cos = _np.tile(_np.cos(ang), (4, 1)).astype(f32)
    sin = _np.tile(_np.concatenate([-_np.sin(ang), _np.sin(ang)]), (2, 1)).astype(f32)
    vec[0:HEAD, 26] = 1.0 / HEAD
    vec[HEAD:P, 27] = 1.0 / HEAD
    mask = _np.triu(_np.full((P, P), MASKED, f32), 1)

    arrays = {
        "x": a["x"].reshape(TT, P, D),
        "wt": _np.stack(tiles),
        "vec": vec,
        "gain2": _np.ascontiguousarray(_np.broadcast_to(a["ffn_norm"][0], (P, D))),
        "lams": _np.ascontiguousarray(_np.broadcast_to(lams, (P, 4 * HEAD))),
        "ident": _np.eye(P, dtype=f32),
        "mask": mask,
        "cos": cos,
        "sin": sin,
    }
    nc = _bacc.Bacc("TRN2", target_bir_lowering=False, num_devices=1)
    args = [nc.dram_tensor(n, v.shape, _mybir.dt.from_np(v.dtype), kind="ExternalInput").ap() for n, v in arrays.items()]
    out = nc.dram_tensor("out", (TT, P, D), _mybir.dt.float32, kind="ExternalOutput").ap()
    build(nc, *args, out)
    r = _run(nc, [arrays], core_ids=[0])
    return r.results[0]["out"].reshape(1, SEQ, D)
```

```python
from contextlib import ExitStack

import concourse.bass as bass
from concourse import mybir

ALU = mybir.AluOpType
ACT = mybir.ActivationFunctionType
AX = mybir.AxisListType
F32 = mybir.dt.float32
F32R = mybir.dt.float32r
U32 = mybir.dt.uint32

P = 128
SEQ = 512
D = 1024
FFN = 2816
HEAD = 64
EPS = 1e-6
BLOCK = 256
TT = SEQ // P
KT = D // P
PAIRS = 8
MOBA_PAIRS = 4
FT = FFN // P
LAMBDA_INIT = 0.8 - 0.6 * 1.0
Q_GAIN, K_GAIN = KT, KT + PAIRS
NEWTON = 3
NEWTON_OPS = 3 + 3 * NEWTON
RSQRT_MAGIC = 0x5F3759DF
MASKED = -(2.0 ** 127)
WARM = 4
OUT_BANKS = ((0, 1, 7, 2), (4, 5, 6, 3))

G_OUT = 3 * PAIRS
G_FFN = G_OUT + KT
G_DOWN = G_FFN + 2 * FT
TILES = G_DOWN + FT
ROUNDS = (TILES - G_FFN) // 4
REST = (TILES - G_FFN) % 4
GATE_ROUNDS = (G_DOWN - G_FFN) // 4

assert G_FFN % 4 == 0 and G_DOWN % 4 == 0
assert SEQ // BLOCK == 2, "MoBA is causal attention for two blocks only"

RING3 = G_OUT + 3
LOADS_BEFORE = (RING3 // 3 + 1, RING3 // 3 + 1, RING3 // 3 + 1, 2)
assert RING3 % 4 == 3


def build(nc, x, wt, vec, gain2, lams, ident_in, mask_in, cos_in, sin_in, out):
    with ExitStack() as ctx:
        cursor = [16512]

        def place(name, shape, dt, at=None):
            n = 4
            for s in shape[1:]:
                n *= s
            if at is None:
                at = cursor[0]
                cursor[0] += n
            return nc.alloc_sbuf_tensor_at(name, shape, dt, offset=at), at

        def sem(name):
            return ctx.enter_context(nc.semaphore(name))

        X, _ = place("residual", [P, TT, D], F32)
        RAW, _ = place("w_raw", [P, 4, D], F32)
        WH, at_wh = place("w_hi", [P, 4, D], F32R)
        WL, at_wl = place("w_lo", [P, 4, D], F32R)
        ident, _ = place("ident", [P, P], F32)
        mask, _ = place("mask", [P, P], F32)
        cosT, _ = place("cos", [P, SEQ], F32)
        sinT, _ = place("sin", [P, SEQ], F32)
        small, _ = place("small", [P, 208], F32)
        QG, at_tmp = place("q_gained", [P, SEQ], F32)
        QR, _ = place("q_rotated", [P, SEQ], F32)
        QS, _ = place("q_roped", [P, SEQ], F32)
        KG, _ = place("k_gained", [P, SEQ], F32)
        KR, _ = place("k_rotated", [P, SEQ], F32)
        KS, _ = place("k_roped", [P, SEQ], F32)
        VT, _ = place("v_by_dim", [P, SEQ], F32)
        SG, _ = place("silu_gate", [P, 2, SEQ], F32, at_tmp)
        AC, _ = place("gated", [P, 2, SEQ], F32, at_tmp + 4096)
        WO, _ = place("w_out_parts", [P, 2, D], F32R, at_tmp)
        KB = 1024
        H1, r0 = place("h_parts", [P, KT, 2, SEQ], F32R)
        MIX, r1 = place("mixed_parts", [P, KT, 2, SEQ], F32R)
        HID, _ = place("hidden_parts", [P, FT, 2, SEQ], F32R, r0)
        r2 = r1 + 32 * KB
        V, _ = place("v_parts", [P, 2, 2, TT, P], F32R, r2)
        VH, VL = V[:, 0], V[:, 1]
        QH, _ = place("q_hi", [P, SEQ], F32R, r2 + 8 * KB)
        QL, _ = place("q_lo", [P, SEQ], F32R, r2 + 10 * KB)
        KH, _ = place("k_hi", [P, SEQ], F32R, r2 + 12 * KB)
        KL, _ = place("k_lo", [P, SEQ], F32R, r2 + 14 * KB)
        SQQ, _ = place("q_squared", [P, SEQ], F32, r2 + 16 * KB)
        SQK, _ = place("k_squared", [P, SEQ], F32, r2 + 18 * KB)
        KBC, _ = place("k_rstd_spread", [P, TT, 2, HEAD], F32, r2 + 20 * KB)
        ON, _ = place("o_normed", [P, TT, P], F32, r2 + 22 * KB)
        LAM0, _ = place("lambda_in", [P, 4 * HEAD], F32, r2 + 22 * KB)
        HN2, _ = place("h2_normed", [P, TT, D], F32, r2)
        JUNK2, _ = place("squares2", [P, D], F32, r2 + 16 * KB)
        G2, _ = place("ffn_gain", [P, D], F32, r2 + 20 * KB)
        r3 = r2 + 24 * KB
        H2, _ = place("h2_parts", [P, KT, 2, SEQ], F32R, r3)
        PTH, _ = place("probsT_hi", [P, 2, TT, SEQ], F32R, r3)
        PTL, _ = place("probsT_lo", [P, 2, TT, SEQ], F32R, r3 + 16 * KB)
        JUNK, _ = place("squares", [P, 2, D], F32, r3 + 16 * KB)
        RB, _ = place("x_rstd_spread", [P, SEQ], F32, r3 + 32 * KB)
        PR0, _ = place("probs_0", [P, 2, SEQ], F32, at_wh + 3 * 4 * D)
        PR1, _ = place("probs_1", [P, 2, SEQ], F32, at_wl + 3 * 4 * D)
        PR = (PR0, PR1)

        VEC = small[:, 0:28]
        IND = small[:, 26:28]
        NA = small[:, 32:48]
        NT = small[:, 48:64]
        NY = small[:, 64:80]
        NZ = small[:, 80:96]
        RQ = small[:, 96:104]
        SUM = small[:, 104:112]
        RS = small[:, 112:120]
        MX = small[:, 120:128]
        NB = small[:, 128:136]
        SS = small[:, 136:140]
        SO = small[:, 140:144]
        LP = small[:, 144:148]
        MLAM = small[:, 148:149]
        SUBG = small[:, 149:150]
        NL = small[:, 152:156]
        S2 = small[:, 156:160]
        EX = small[:, 160:176]
        EO = small[:, 176:180]

        ps = ctx.enter_context(nc.psum_tensor("ps", [P, 8, SEQ], F32))

        x_in = [sem(f"x_in{t}") for t in range(TT)]
        ident_in_s = sem("ident_in")
        small_in = sem("small_in")
        rope_in = sem("rope_in")
        misc_in = sem("misc_in")
        gain2_in = sem("gain2_in")
        raw_in = [sem(f"raw_in{s}") for s in range(4)]
        w_hi = sem("w_hi_ready")
        w_lo = sem("w_lo_ready")
        w_used = sem("w_used")
        x_sq = sem("x_squared")
        x_sq_dve = sem("x_squared_dve")
        x_newton = sem("x_newton_step")
        qk_newton = sem("qk_newton_step")
        o_newton = sem("o_newton_step")
        h2_newton = sem("h2_newton_step")
        ex_ready = sem("eps_scaled")
        rb_copied = sem("x_rstd_copied")
        rb_turned = sem("x_rstd_turned")
        rb_s = sem("x_rstd_spread_ready")
        s2_s = sem("residual_squared")
        hn = sem("h2_normed")
        x_turned = sem("x_turned")
        hh = sem("h_hi_ready")
        hl = sem("h_lo_ready")
        lam_dot = sem("lambda_dots")
        lam_exp = sem("lambda_exps")
        lam_step = sem("lambda_step")
        lam_s = sem("lambda_ready")
        pads = sem("v_pads_cleared")
        q_ev = sem("q_evacuated")
        k_ev = sem("k_evacuated")
        v_ev = sem("v_evacuated")
        v_scaled = sem("v_scaled")
        q_rot = sem("q_rotated_in")
        k_rot = sem("k_rotated_in")
        q_pool = sem("q_rope_step")
        k_pool = sem("k_rope_step")
        qh_s, ql_s, kh_s, kl_s = sem("q_hi_ready"), sem("q_lo_ready"), sem("k_hi_ready"), sem("k_lo_ready")
        kn_s = sem("k_normed")
        ms_s = sem("mean_squares")
        rq_s = sem("q_scale_ready")
        kbc_s = sem("k_rstd_spread_ready")
        kb_s = sem("k_rstd_turned")
        v_turn = sem("v_turned")
        vh_s, vl_s = sem("v_hi_ready"), sem("v_lo_ready")
        sc_s = sem("scores_ready")
        masked = sem("scores_masked")
        mx_s = sem("max_found")
        nb_s = sem("bias_ready")
        ex_s = sem("exp_ready")
        rs_s = sem("sums_inverted")
        lr_s = sem("map1_scale_ready")
        eo_s = sem("o_eps_ready")
        pn_s = sem("probs_normed")
        pt_s = sem("probs_turned")
        ph_s, pl_s = sem("probsT_hi_ready"), sem("probsT_lo_ready")
        pv_s = sem("heads_out")
        o_main = sem("o_first_part")
        o_add = sem("o_added")
        o_sq = sem("o_squared")
        on_s = sem("o_normed_ready")
        o_turn = sem("o_turned")
        mh_s, ml_s = sem("mixed_hi_ready"), sem("mixed_lo_ready")
        wo_s = sem("out_rows")
        res = sem("residual_added")
        h2_turned = sem("h2_turned")
        h2h, h2l = sem("h2_hi_ready"), sem("h2_lo_ready")
        silu_s, gated_s = sem("silu_ready"), sem("gated_ready")
        ah_s, al_s = sem("hidden_hi_ready"), sem("hidden_lo_ready")
        y_done = sem("down_rows")
        y_add = sem("output_added")
        stored = sem("stored")


        def from_(t, n):
            return not isinstance(t, int) or t >= n

        def turned(t, qt, a, moba):
            if moba:
                return t * 8 + (2 * qt + a + 1)
            return t * 4 + (4 * MOBA_PAIRS + qt + 1)

        def maps(moba):
            return range(2) if moba else range(1)

        def o_columns(qt):
            c = qt % 2 * 2 * P
            return slice(c, c + P), slice(c + P, c + 2 * P)

        def round_w_used(r, n):
            return r * 4 + (G_OUT + n + 1)

        block = ctx.enter_context(nc.Block())

        @block.sync
        def _(sp):
            def load(g, slot, back):
                if back:
                    sp.wait_ge(w_lo, g - (back - 1))
                sp.dma_start(RAW[:, slot], wt[g]).then_inc(raw_in[slot], 16)

            def rotate(dst, src, evac, pool, done, p):
                sp.wait_ge(evac, p * 2 + 2)
                if from_(p, 1):
                    sp.wait_ge(pool, p * 3)
                for b in range(4):
                    sp.dma_start(dst[32 * b:32 * b + 32], src[32 * (b ^ 1):32 * (b ^ 1) + 32]).then_inc(done, 16)

            for t in range(TT):
                sp.dma_start(X[:, t], x[t]).then_inc(x_in[t], 16)
                if t == 0:
                    sp.dma_start(ident[:], ident_in).then_inc(ident_in_s, 16)
                    sp.dma_start(small[:, 0:28], vec).then_inc(small_in, 16)
            load(0, 0, 0)
            sp.dma_start(mask[:], mask_in).then_inc(misc_in, 16)
            sp.dma_start(LAM0[:], lams).then_inc(misc_in, 16)
            load(1, 1, 0)
            sp.dma_start(cosT[:], cos_in).then_inc(rope_in, 16)
            sp.dma_start(sinT[:], sin_in).then_inc(rope_in, 16)
            load(2, 2, 0)

            def pair_loads(p):
                load(p * 3 + 3, 0, 3)
                rotate(QR, QG, q_ev, q_pool, q_rot, p)
                load(p * 3 + 4, 1, 3)
                rotate(KR, KG, k_ev, k_pool, k_rot, p)
                load(p * 3 + 5, 2, 3)

            pair_loads(0)
            with sp.Fori(1, PAIRS) as p:
                pair_loads(p)
            load(RING3, 3, 0)
            for g in range(RING3 + 1, G_FFN):
                load(g, g % 4, 4)
            sp.wait_ge(o_turn, PAIRS - MOBA_PAIRS)
            sp.dma_start(G2[:], gain2).then_inc(gain2_in, 16)
            with sp.Fori(0, ROUNDS) as r:
                for n in range(4):
                    load(r * 4 + (G_FFN + n), n, 4)
            for n in range(REST):
                load(4 * ROUNDS + G_FFN + n, n, 4)
            for tt in range(TT):
                for half in range(2):
                    sp.wait_ge(y_add, 2 * tt + half + 1)
                    sp.dma_start(out[tt, :, half * SEQ:(half + 1) * SEQ],
                                 X[:, tt, half * SEQ:(half + 1) * SEQ]).then_inc(stored, 16)
            sp.wait_ge(stored, 16 * 2 * TT)

        @block.gpsimd
        def _(pool):
            def scale_v(p):
                pool.wait_ge(v_ev, p + 1)
                nc.gpsimd.tensor_tensor(VT[:], VT[:], RB[:], ALU.mult).then_inc(v_scaled, 1)

            def rope(p, G, R, S, ev, rot, step, hi, lo):
                pool.wait_ge(ev, p * 2 + 2)
                if from_(p, 1):
                    pool.wait_ge(hi, p)
                    pool.wait_ge(lo, p)
                nc.gpsimd.tensor_tensor(S[:], G[:], cosT[:], ALU.mult).then_inc(step, 1)
                pool.wait_ge(rot, p * 64 + 64)
                nc.gpsimd.tensor_tensor(R[:], R[:], sinT[:], ALU.mult).then_inc(step, 1)
                pool.wait_ge(step, p * 3 + 2)
                nc.gpsimd.tensor_tensor(S[:], S[:], R[:], ALU.add).then_inc(step, 1)

            nc.gpsimd.memset(VH[:, 0, :, HEAD:P].bitcast(F32), 0.0)
            nc.gpsimd.memset(VH[:, 1, :, 0:HEAD].bitcast(F32), 0.0)
            nc.gpsimd.memset(VL[:, 0, :, HEAD:P].bitcast(F32), 0.0)
            nc.gpsimd.memset(VL[:, 1, :, 0:HEAD].bitcast(F32), 0.0).then_inc(pads, 1)
            pool.wait_ge(rope_in, 32)
            rope(0, QG, QR, QS, q_ev, q_rot, q_pool, qh_s, ql_s)
            rope(0, KG, KR, KS, k_ev, k_rot, k_pool, kh_s, kl_s)
            pool.wait_ge(rb_s, 1)
            scale_v(0)
            with pool.Fori(1, PAIRS) as p:
                rope(p, QG, QR, QS, q_ev, q_rot, q_pool, qh_s, ql_s)
                rope(p, KG, KR, KS, k_ev, k_rot, k_pool, kh_s, kl_s)
                scale_v(p)

        @block.scalar
        def _(act):
            def split_hi(slot, loads):
                act.wait_ge(raw_in[slot], loads * 16)
                nc.scalar.activation(WH[:, slot], RAW[:, slot], ACT.Copy).then_inc(w_hi, 1)

            def project_hi(p, j):
                if from_(p, 1) or j >= 3:
                    act.wait_ge(w_used, p * 3 + (j - 2))
                split_hi(j % 3, p + (j // 3 + 1))

            def out_hi(g):
                if g == RING3:
                    act.wait_ge(raw_in[3], 16)
                    act.wait_ge(ql_s, PAIRS)
                    act.wait_ge(k_pool, 3 * PAIRS)
                    nc.scalar.activation(WO[:, 0], RAW[:, 3], ACT.Copy).then_inc(w_hi, 1)
                else:
                    k = 2 * (g - RING3 - 1)
                    act.wait_ge(raw_in[g % 4], 16 * LOADS_BEFORE[g % 4])
                    act.wait_ge(w_used, G_OUT)
                    nc.scalar.activation(H1[:, k:k + 2, 0], RAW[:, g % 4].rearrange("p (k n) -> p k n", k=2),
                                         ACT.Copy).then_inc(w_hi, 1)

            def ffn_hi(r, n):
                if isinstance(r, int) and r == 0:
                    act.wait_ge(wo_s, TT)
                else:
                    act.wait_ge(w_used, round_w_used(r - 1, n))
                split_hi(n, r + (LOADS_BEFORE[n] + 1))

            def evacuate(p, j, bank, SQ, G, ev, col, evs, o_used):
                act.wait_ge(w_used, p * 3 + (j + 1))
                if from_(p, 1):
                    act.wait_ge(ms_s, p)
                if o_used:
                    act.wait_ge(o_sq, p - (MOBA_PAIRS + 1))
                nc.scalar.activation(SQ[:], ps[:, bank], ACT.Square).then_inc(ev, 1)
                if from_(p, 1):
                    act.wait_ge(evs, p * 3)
                nc.scalar.activation(G[:], ps[:, bank], ACT.Copy, scale=VEC[:, bass.ds(p + col, 1)]).then_inc(ev, 1)

            def q_evac(p, o_used):
                evacuate(p, 0, 0, SQQ, QG, q_ev, Q_GAIN, q_pool, o_used)

            def k_evac(p, o_used):
                evacuate(p, 1, 1, SQK, KG, k_ev, K_GAIN, k_pool, o_used)

            def v_evac(p):
                act.wait_ge(w_used, p * 3 + 3)
                if from_(p, 1):
                    act.wait_ge(v_turn, p)
                nc.scalar.activation(VT[:], ps[:, 0], ACT.Copy).then_inc(v_ev, 1)

            def q_hi(p):
                act.wait_ge(q_pool, p * 3 + 3)
                if from_(p, 1):
                    act.wait_ge(sc_s, p * 4)
                nc.scalar.activation(QH[:], QS[:], ACT.Copy).then_inc(qh_s, 1)

            def k_hi(p):
                act.wait_ge(kn_s, p + 1)
                if from_(p, 1):
                    act.wait_ge(sc_s, p * 4)
                nc.scalar.activation(KH[:], KS[:], ACT.Copy).then_inc(kh_s, 1)

            def v_hi(t, moba):
                act.wait_ge(v_turn, t + 1)
                act.wait_ge(pads, 1)
                if from_(t, 1):
                    act.wait_ge(pv_s, t)
                turned_v = ps[:, 7].rearrange("p (t d) -> p t d", t=TT)
                if moba:
                    nc.scalar.activation(VH[:, 0, :, 0:HEAD], turned_v[:, :, 0:HEAD], ACT.Copy)
                    nc.scalar.activation(VH[:, 1, :, HEAD:P], turned_v[:, :, HEAD:P], ACT.Copy).then_inc(vh_s, 1)
                else:
                    nc.scalar.activation(VH[:, 0], turned_v, ACT.Copy).then_inc(vh_s, 1)

            def exps(t, qt, moba):
                W = (qt + 1) * P
                act.wait_ge(nb_s, t * 4 + (qt + 1))
                for a in range(2):
                    i = 2 * qt + a
                    if qt >= 2:
                        act.wait_ge(pt_s, turned(t, qt - 2, a, moba))
                    elif from_(t, 1):
                        moba_before = t - 1 < MOBA_PAIRS if isinstance(t, int) else moba
                        act.wait_ge(pt_s, turned(t - 1, qt + 2, a, moba_before))
                    nc.scalar.activation(PR[qt % 2][:, a, 0:W], ps[:, 2 + a, 0:W], ACT.Exp, bias=NB[:, i:i + 1],
                                         scale=RQ[:, i:i + 1], accum_out=SUM[:, i:i + 1]).then_inc(ex_s, 1)

            def pt_hi(t, qt, moba):
                for a in maps(moba):
                    act.wait_ge(pt_s, turned(t, qt, a, moba))
                    if from_(t, 1):
                        act.wait_ge(pv_s, t)
                    bank = 4 + (a if moba else qt % 2)
                    nc.scalar.activation(PTH[:, a, 0:qt + 1, qt * P:(qt + 1) * P],
                                         ps[:, bank, 0:(qt + 1) * P].rearrange("p (k q) -> p k q", q=P),
                                         ACT.Copy).then_inc(ph_s, 1)

            def o_copy(t):
                act.wait_ge(pv_s, t + 1)
                parts = ps[:, 5:7].rearrange("p b (q c d) -> p (b q) c d", q=2, c=2)
                nc.scalar.activation(ON[:], parts[:, :, 0], ACT.Copy).then_inc(o_main, 1)

            def o_squares(t):
                act.wait_ge(o_add, t - (MOBA_PAIRS - 1))
                act.wait_ge(ms_s, min(t + 2, PAIRS) if isinstance(t, int) else t + 2)
                for qt in range(TT):
                    qs = slice(qt * P, (qt + 1) * P)
                    ins = nc.scalar.activation(SQQ[:, qs], ON[:, qt], ACT.Square, accum_out=SO[:, qt:qt + 1])
                ins.then_inc(o_sq, 1)

            def mix_hi(t, moba):
                if moba:
                    act.wait_ge(pv_s, t + 1)
                    nc.scalar.activation(MIX[:, t, 0], ps[:, 6], ACT.Copy).then_inc(mh_s, 1)
                else:
                    act.wait_ge(o_turn, t - (MOBA_PAIRS - 1))
                    nc.scalar.activation(MIX[:, t, 0], ps[:, 6], ACT.Copy, scale=SUBG).then_inc(mh_s, 1)

            for n, t in enumerate((0, 2)):
                act.wait_ge(x_in[t], 16)
                if n == 1:
                    act.wait_ge(x_sq, 1)
                nc.scalar.activation(JUNK[:, 0], X[:, t], ACT.Square, accum_out=SS[:, t:t + 1]).then_inc(x_sq, 1)
            project_hi(0, 0)
            act.wait_ge(small_in, 16)
            for k in range(KT):
                act.wait_ge(x_turned, k + 1)
                nc.scalar.activation(H1[:, k, 0], ps[:, k], ACT.Copy, scale=VEC[:, k:k + 1]).then_inc(hh, 1)
            project_hi(0, 1)
            project_hi(0, 2)
            q_evac(0, False)
            act.wait_ge(rb_turned, 1)
            nc.scalar.activation(RB[:], ps[:, 7], ACT.Copy).then_inc(rb_s, 1)
            project_hi(0, 3)
            act.wait_ge(lam_dot, 2)
            nc.scalar.activation(LP[:, 2:4], LP[:, 0:2], ACT.Exp).then_inc(lam_exp, 1)
            k_evac(0, False)
            q_hi(0)
            v_evac(0)
            k_hi(0)
            project_hi(0, 4)
            v_hi(0, True)
            exps(0, 0, True)
            project_hi(1, 2)
            exps(0, 1, True)
            pt_hi(0, 0, True)
            q_evac(1, False)
            pt_hi(0, 1, True)
            exps(0, 2, True)
            project_hi(1, 3)
            k_evac(1, False)
            exps(0, 3, True)
            pt_hi(0, 2, True)
            q_hi(1)
            pt_hi(0, 3, True)
            v_evac(1)
            project_hi(1, 4)
            k_hi(1)
            mix_hi(0, True)
            with act.Fori(1, MOBA_PAIRS) as t:
                exps(t, 0, True)
                v_hi(t, True)
                pt_hi(t, 0, True)
                exps(t, 1, True)
                project_hi(t + 1, 2)
                project_hi(t + 1, 3)
                exps(t, 2, True)
                pt_hi(t, 1, True)
                q_evac(t + 1, False)
                exps(t, 3, True)
                k_evac(t + 1, False)
                pt_hi(t, 2, True)
                pt_hi(t, 3, True)
                project_hi(t + 1, 4)
                q_hi(t + 1)
                k_hi(t + 1)
                v_evac(t + 1)
                mix_hi(t, True)
            project_hi(5, 2)
            exps(4, 0, False)
            pt_hi(4, 0, False)
            exps(4, 1, False)
            v_hi(4, False)
            exps(4, 2, False)
            project_hi(5, 3)
            q_evac(5, False)
            pt_hi(4, 1, False)
            exps(4, 3, False)
            k_evac(5, False)
            pt_hi(4, 2, False)
            pt_hi(4, 3, False)
            q_hi(5)
            project_hi(5, 4)
            v_evac(5)
            k_hi(5)
            with act.Fori(MOBA_PAIRS + 1, PAIRS - 1) as t:
                project_hi(t + 1, 2)
                o_copy(t - 1)
                exps(t, 0, False)
                pt_hi(t, 0, False)
                exps(t, 1, False)
                o_squares(t - 1)
                v_hi(t, False)
                exps(t, 2, False)
                project_hi(t + 1, 3)
                q_evac(t + 1, True)
                pt_hi(t, 1, False)
                exps(t, 3, False)
                k_evac(t + 1, True)
                pt_hi(t, 2, False)
                mix_hi(t - 1, False)
                pt_hi(t, 3, False)
                q_hi(t + 1)
                project_hi(t + 1, 4)
                v_evac(t + 1)
                k_hi(t + 1)
            v_hi(7, False)
            o_copy(6)
            project_hi(8, 2)
            o_squares(6)
            exps(7, 0, False)
            exps(7, 1, False)
            pt_hi(7, 0, False)
            exps(7, 2, False)
            pt_hi(7, 1, False)
            out_hi(G_OUT + 3)
            mix_hi(6, False)
            exps(7, 3, False)
            pt_hi(7, 2, False)
            pt_hi(7, 3, False)
            out_hi(G_OUT + 4)
            for g in range(G_OUT + 5, G_FFN):
                out_hi(g)
            o_copy(PAIRS - 1)
            o_squares(PAIRS - 1)
            mix_hi(PAIRS - 1, False)

            def h2_hi(tt):
                act.wait_ge(h2_turned, tt + 1)
                nc.scalar.activation(H2[:, :, 0, tt * P:(tt + 1) * P],
                                     ps[:, 0:2].rearrange("p b (k q) -> p (b k) q", q=P),
                                     ACT.Copy).then_inc(h2h, 1)

            for tt in range(TT):
                act.wait_ge(res, TT + tt + 1)
                if tt >= 1:
                    act.wait_ge(s2_s, tt)
                nc.scalar.activation(JUNK2[:], X[:, tt], ACT.Square, accum_out=S2[:, tt:tt + 1]).then_inc(s2_s, 1)
                ffn_hi(0, tt)
                if tt >= 1:
                    h2_hi(tt - 1)
            h2_hi(TT - 1)

            def silu(f, par):
                act.wait_ge(w_used, f * 2 + (G_OUT + 1))
                if from_(f, 2):
                    act.wait_ge(gated_s, f - 1)
                nc.scalar.activation(SG[:, par], ps[:, 4 + 2 * par], ACT.Silu).then_inc(silu_s, 1)

            def hidden_hi(f, par):
                act.wait_ge(gated_s, f + 1)
                nc.scalar.activation(HID[:, f, 0], AC[:, par], ACT.Copy).then_inc(ah_s, 1)

            def hidden_round(r):
                for par in range(2):
                    silu(r * 2 + par, par)
                    ffn_hi(r + 1, 2 * par)
                    hidden_hi(r * 2 + par, par)
                    ffn_hi(r + 1, 2 * par + 1)

            hidden_round(0)
            with act.Fori(1, GATE_ROUNDS) as r:
                hidden_round(r)
            with act.Fori(GATE_ROUNDS + 1, ROUNDS) as r:
                for n in range(4):
                    ffn_hi(r, n)
            for n in range(REST):
                ffn_hi(ROUNDS, n)

        @block.vector
        def _(dve):
            def step(ins, chain, n):
                ins.then_inc(chain, 1)
                dve.wait_ge(chain, n)

            def rsqrt(src, n, scale, chain, turn, eps=None):
                a, h, y, z = (v[:, 0:n] for v in (NA, NT, NY, NZ))
                at = turn * NEWTON_OPS
                if eps is None:
                    step(nc.vector.tensor_scalar(a, src, scale, EPS, ALU.mult, ALU.add), chain, at + 1)
                else:
                    step(nc.vector.scalar_tensor_tensor(out=a, in0=src, scalar=scale, in1=eps, op0=ALU.mult,
                                                        op1=ALU.add), chain, at + 1)
                step(nc.vector.tensor_scalar(h.bitcast(U32), a.bitcast(U32), 1, None, ALU.logical_shift_right),
                     chain, at + 2)
                step(nc.vector.tensor_scalar(y.bitcast(U32), h.bitcast(U32), -1.0, float(RSQRT_MAGIC),
                                             ALU.mult, ALU.add), chain, at + 3)
                for i in range(NEWTON):
                    step(nc.vector.tensor_tensor(z, y, y, ALU.mult), chain, at + (3 * i + 4))
                    step(nc.vector.scalar_tensor_tensor(out=z, in0=z, scalar=-0.5, in1=a, op0=ALU.mult, op1=ALU.mult),
                         chain, at + (3 * i + 5))
                    step(nc.vector.scalar_tensor_tensor(out=y, in0=z, scalar=1.5, in1=y, op0=ALU.add, op1=ALU.mult),
                         chain, at + (3 * i + 6))
                return y

            def split_lo(slot, n):
                dve.wait_ge(w_hi, n)
                nc.vector.tensor_tensor(WL[:, slot], RAW[:, slot], WH[:, slot].bitcast(F32),
                                        ALU.subtract).then_inc(w_lo, 1)

            def project_lo(p, j):
                split_lo(j % 3, p * 3 + (j + 1))

            def out_lo(g):
                dve.wait_ge(w_hi, g + 1)
                if g == RING3:
                    nc.vector.tensor_tensor(WO[:, 1], RAW[:, 3], WO[:, 0].bitcast(F32), ALU.subtract).then_inc(w_lo, 1)
                else:
                    k = 2 * (g - RING3 - 1)
                    nc.vector.tensor_tensor(H1[:, k:k + 2, 1], RAW[:, g % 4].rearrange("p (k n) -> p k n", k=2),
                                            H1[:, k:k + 2, 0].bitcast(F32), ALU.subtract).then_inc(w_lo, 1)

            def ffn_lo(r, n):
                split_lo(n, r * 4 + (G_FFN + n + 1))

            def q_lo(p):
                dve.wait_ge(qh_s, p + 1)
                nc.vector.tensor_tensor(QL[:], QS[:], QH[:].bitcast(F32), ALU.subtract).then_inc(ql_s, 1)

            def scales(p):
                dve.wait_ge(ms_s, p + 1)
                if not from_(p, 1):
                    dve.wait_ge(ex_ready, 1)
                    dve.wait_ge(rb_turned, 1)
                y = rsqrt(ps[:, 7, 0:16], 16, 1.0, qk_newton, p, EX)
                if from_(p, 1):
                    dve.wait_ge(ex_s, p * 8)
                nc.vector.tensor_scalar(RQ, y[:, 0:8], HEAD ** -0.5, None, ALU.mult).then_inc(rq_s, 1)
                if from_(p, 1):
                    dve.wait_ge(kb_s, p)
                nc.vector.tensor_copy(KBC[:].rearrange("p t a e -> p (t a) e"),
                                      y[:, 8:16].unsqueeze(2).broadcast_to([P, 8, HEAD])).then_inc(kbc_s, 1)

            def k_norm(p):
                dve.wait_ge(kb_s, p + 1)
                dve.wait_ge(k_pool, p * 3 + 3)
                nc.vector.tensor_tensor(KS[:], KS[:], ps[:, 7], ALU.mult).then_inc(kn_s, 1)
                dve.wait_ge(kh_s, p + 1)
                nc.vector.tensor_tensor(KL[:], KS[:], KH[:].bitcast(F32), ALU.subtract).then_inc(kl_s, 1)

            def v_lo(t, moba):
                dve.wait_ge(vh_s, t + 1)
                turned_v = ps[:, 7].rearrange("p (t d) -> p t d", t=TT)
                if moba:
                    nc.vector.tensor_tensor(VL[:, 0, :, 0:HEAD], turned_v[:, :, 0:HEAD],
                                            VH[:, 0, :, 0:HEAD].bitcast(F32), ALU.subtract)
                    nc.vector.tensor_tensor(VL[:, 1, :, HEAD:P], turned_v[:, :, HEAD:P],
                                            VH[:, 1, :, HEAD:P].bitcast(F32), ALU.subtract).then_inc(vl_s, 1)
                else:
                    nc.vector.tensor_tensor(VL[:, 0], turned_v, VH[:, 0].bitcast(F32), ALU.subtract).then_inc(vl_s, 1)

            def maxima(t, qt):
                W = (qt + 1) * P
                n = t * 4 + (qt + 1)
                i = slice(2 * qt, 2 * qt + 2)
                diagonal = ps[:, 2:4, qt * P:W]
                dve.wait_ge(sc_s, n)
                nc.vector.tensor_tensor(diagonal, diagonal, mask[:].unsqueeze(1).broadcast_to([P, 2, P]),
                                        ALU.add).then_inc(masked, 1)
                dve.wait_ge(masked, n)
                nc.vector.tensor_reduce(MX[:, i], ps[:, 2:4, 0:W], AX.X, ALU.max).then_inc(mx_s, 1)
                dve.wait_ge(mx_s, n)
                dve.wait_ge(rq_s, t + 1)
                nc.vector.scalar_tensor_tensor(out=NB[:, i], in0=MX[:, i], scalar=-1.0, in1=RQ[:, i], op0=ALU.mult,
                                               op1=ALU.mult).then_inc(nb_s, 1)

            def norm(t, qt, moba):
                W = (qt + 1) * P
                i = 2 * qt
                p0, p1 = PR[qt % 2][:, 0, 0:W], PR[qt % 2][:, 1, 0:W]
                dve.wait_ge(ex_s, t * 8 + (i + 2))
                nc.vector.reciprocal(RS[:, i:i + 2], SUM[:, i:i + 2]).then_inc(rs_s, 1)
                dve.wait_ge(rs_s, t * 4 + (qt + 1))
                if moba:
                    nc.vector.tensor_scalar(p0, p0, RS[:, i:i + 1], None, ALU.mult).then_inc(pn_s, 1)
                    nc.vector.tensor_scalar(p1, p1, RS[:, i + 1:i + 2], None, ALU.mult).then_inc(pn_s, 1)
                else:
                    nc.vector.scalar_tensor_tensor(out=NL[:, qt:qt + 1], in0=SUM[:, i:i + 1], scalar=MLAM,
                                                   in1=RS[:, i + 1:i + 2], op0=ALU.mult, op1=ALU.mult).then_inc(lr_s, 1)
                    dve.wait_ge(lr_s, t * 4 + (qt + 1 - 4 * MOBA_PAIRS))
                    nc.vector.scalar_tensor_tensor(out=p0, in0=p1, scalar=NL[:, qt:qt + 1], in1=p0,
                                                   op0=ALU.mult, op1=ALU.add).then_inc(pn_s, 1)
                    if qt == TT - 1:
                        sums = SUM.rearrange("p (t a) -> p t a", a=2)[:, :, 0]
                        nc.vector.scalar_tensor_tensor(out=EO, in0=sums, scalar=EPS, in1=sums, op0=ALU.mult,
                                                       op1=ALU.mult).then_inc(eo_s, 1)

            def pt_lo(t, qt, moba):
                for a in maps(moba):
                    dve.wait_ge(ph_s, turned(t, qt, a, moba))
                    bank = 4 + (a if moba else qt % 2)
                    at = (slice(None), a, slice(0, qt + 1), slice(qt * P, (qt + 1) * P))
                    nc.vector.tensor_tensor(PTL[at], ps[:, bank, 0:(qt + 1) * P].rearrange("p (k q) -> p k q", q=P),
                                            PTH[at].bitcast(F32), ALU.subtract).then_inc(pl_s, 1)

            def o_sum(t):
                dve.wait_ge(o_main, t - (MOBA_PAIRS - 1))
                parts = ps[:, 5:7].rearrange("p b (q c d) -> p (b q) c d", q=2, c=2)
                nc.vector.tensor_tensor(ON[:], parts[:, :, 1], ON[:], ALU.add).then_inc(o_add, 1)

            def o_norm(t):
                dve.wait_ge(o_sq, t - (MOBA_PAIRS - 1))
                dve.wait_ge(eo_s, t - (MOBA_PAIRS - 1))
                y = rsqrt(SO, TT, 1.0 / P, o_newton, t - MOBA_PAIRS, EO)
                nc.vector.tensor_tensor(ON[:], ON[:], y.unsqueeze(2).broadcast_to([P, TT, P]),
                                        ALU.mult).then_inc(on_s, 1)

            def mix_lo(t, moba):
                dve.wait_ge(mh_s, t + 1)
                if moba:
                    nc.vector.tensor_tensor(MIX[:, t, 1], ps[:, 6], MIX[:, t, 0].bitcast(F32),
                                            ALU.subtract).then_inc(ml_s, 1)
                else:
                    nc.vector.scalar_tensor_tensor(out=MIX[:, t, 1], in0=ps[:, 6], scalar=SUBG,
                                                   in1=MIX[:, t, 0].bitcast(F32), op0=ALU.mult,
                                                   op1=ALU.subtract).then_inc(ml_s, 1)

            for n, t in enumerate((1, 3)):
                dve.wait_ge(x_in[t], 16)
                if n == 1:
                    dve.wait_ge(x_sq_dve, 1)
                nc.vector.scalar_tensor_tensor(out=JUNK[:, 1], in0=X[:, t], scalar=1.0, in1=X[:, t], op0=ALU.mult,
                                               op1=ALU.mult, accum_out=SS[:, t:t + 1]).then_inc(x_sq_dve, 1)
            project_lo(0, 0)
            dve.wait_ge(small_in, 16)
            for k in range(KT):
                dve.wait_ge(hh, k + 1)
                nc.vector.scalar_tensor_tensor(out=H1[:, k, 1], in0=ps[:, k], scalar=VEC[:, k:k + 1],
                                               in1=H1[:, k, 0].bitcast(F32), op0=ALU.mult,
                                               op1=ALU.subtract).then_inc(hl, 1)
            project_lo(0, 1)
            dve.wait_ge(x_sq, 2)
            dve.wait_ge(x_sq_dve, 2)
            y = rsqrt(SS, TT, 1.0 / D, x_newton, 0)
            nc.vector.tensor_scalar(EX.rearrange("p (j t a) -> p j t a", j=2, t=TT),
                                    NA[:, 0:TT].unsqueeze(1).unsqueeze(3).broadcast_to([P, 2, TT, 2]), EPS, None,
                                    ALU.mult).then_inc(ex_ready, 1)
            nc.vector.tensor_copy(KBC[:].rearrange("p t a e -> p t (a e)"),
                                  y.unsqueeze(2).broadcast_to([P, TT, P])).then_inc(rb_copied, 1)
            project_lo(0, 2)
            dve.wait_ge(misc_in, 32)
            for j in range(2):
                step(nc.vector.tensor_tensor(LAM0[:, 2 * j * HEAD:(2 * j + 1) * HEAD],
                                             LAM0[:, 2 * j * HEAD:(2 * j + 1) * HEAD],
                                             LAM0[:, (2 * j + 1) * HEAD:(2 * j + 2) * HEAD], ALU.mult),
                     lam_step, j + 1)
                nc.vector.tensor_reduce(LP[:, j:j + 1], LAM0[:, 2 * j * HEAD:(2 * j + 1) * HEAD], AX.X,
                                        ALU.add).then_inc(lam_dot, 1)
            nc.vector.tensor_scalar(SUBG, VEC[:, 24:25], 1.0 - LAMBDA_INIT, None, ALU.mult)
            dve.wait_ge(lam_exp, 1)
            step(nc.vector.tensor_tensor(MLAM, LP[:, 3:4], LP[:, 2:3], ALU.subtract), lam_step, 3)
            nc.vector.tensor_scalar(MLAM, MLAM, -LAMBDA_INIT, None, ALU.add).then_inc(lam_s, 1)
            project_lo(0, 3)
            scales(0)
            q_lo(0)
            k_norm(0)
            project_lo(0, 4)
            dve.wait_ge(lam_s, 1)
            maxima(0, 0)
            norm(0, 0, True)
            maxima(0, 1)
            v_lo(0, True)
            norm(0, 1, True)
            pt_lo(0, 0, True)
            maxima(0, 2)
            project_lo(1, 2)
            pt_lo(0, 1, True)
            norm(0, 2, True)
            maxima(0, 3)
            project_lo(1, 3)
            norm(0, 3, True)
            pt_lo(0, 2, True)
            q_lo(1)
            pt_lo(0, 3, True)
            scales(1)
            project_lo(1, 4)
            k_norm(1)
            mix_lo(0, True)
            with dve.Fori(1, MOBA_PAIRS) as t:
                maxima(t, 0)
                norm(t, 0, True)
                maxima(t, 1)
                norm(t, 1, True)
                maxima(t, 2)
                pt_lo(t, 0, True)
                project_lo(t + 1, 2)
                norm(t, 2, True)
                v_lo(t, True)
                maxima(t, 3)
                project_lo(t + 1, 3)
                pt_lo(t, 1, True)
                norm(t, 3, True)
                pt_lo(t, 2, True)
                pt_lo(t, 3, True)
                scales(t + 1)
                q_lo(t + 1)
                k_norm(t + 1)
                project_lo(t + 1, 4)
                mix_lo(t, True)
            maxima(4, 0)
            norm(4, 0, False)
            maxima(4, 1)
            project_lo(5, 2)
            norm(4, 1, False)
            maxima(4, 2)
            pt_lo(4, 0, False)
            maxima(4, 3)
            v_lo(4, False)
            norm(4, 2, False)
            norm(4, 3, False)
            pt_lo(4, 1, False)
            pt_lo(4, 2, False)
            project_lo(5, 3)
            pt_lo(4, 3, False)
            scales(5)
            q_lo(5)
            k_norm(5)
            project_lo(5, 4)
            with dve.Fori(MOBA_PAIRS + 1, PAIRS - 1) as t:
                maxima(t, 0)
                o_sum(t - 1)
                norm(t, 0, False)
                maxima(t, 1)
                project_lo(t + 1, 2)
                norm(t, 1, False)
                maxima(t, 2)
                pt_lo(t, 0, False)
                o_norm(t - 1)
                maxima(t, 3)
                v_lo(t, False)
                norm(t, 2, False)
                norm(t, 3, False)
                pt_lo(t, 1, False)
                pt_lo(t, 2, False)
                mix_lo(t - 1, False)
                project_lo(t + 1, 3)
                pt_lo(t, 3, False)
                scales(t + 1)
                q_lo(t + 1)
                k_norm(t + 1)
                project_lo(t + 1, 4)
            o_sum(6)
            maxima(7, 0)
            project_lo(8, 2)
            v_lo(7, False)
            maxima(7, 1)
            norm(7, 0, False)
            norm(7, 1, False)
            maxima(7, 2)
            o_norm(6)
            maxima(7, 3)
            pt_lo(7, 0, False)
            pt_lo(7, 1, False)
            norm(7, 2, False)
            mix_lo(6, False)
            norm(7, 3, False)
            out_lo(G_OUT + 3)
            pt_lo(7, 2, False)
            pt_lo(7, 3, False)
            out_lo(G_OUT + 4)
            out_lo(G_OUT + 5)
            out_lo(G_OUT + 6)
            o_sum(PAIRS - 1)
            out_lo(G_OUT + 7)
            o_norm(PAIRS - 1)
            mix_lo(PAIRS - 1, False)

            def add_residual(half, tt):
                dve.wait_ge(wo_s, TT * half + tt + 1)
                at = (slice(None), tt, slice(half * SEQ, (half + 1) * SEQ))
                nc.vector.tensor_tensor(X[at], ps[:, OUT_BANKS[half][tt]], X[at], ALU.add).then_inc(res, 1)

            def h2_lo(tt):
                dve.wait_ge(h2h, tt + 1)
                qs = slice(tt * P, (tt + 1) * P)
                nc.vector.tensor_tensor(H2[:, :, 1, qs], ps[:, 0:2].rearrange("p b (k q) -> p (b k) q", q=P),
                                        H2[:, :, 0, qs].bitcast(F32), ALU.subtract).then_inc(h2l, 1)

            for tt in range(TT):
                add_residual(0, tt)
            dve.wait_ge(gain2_in, 16)
            for tt in range(TT):
                add_residual(1, tt)
                if tt >= 1:
                    ffn_lo(0, tt - 1)
                dve.wait_ge(s2_s, tt + 1)
                y = rsqrt(S2[:, tt:tt + 1], 1, 1.0 / D, h2_newton, tt)
                nc.vector.scalar_tensor_tensor(out=HN2[:, tt], in0=X[:, tt], scalar=y, in1=G2[:], op0=ALU.mult,
                                               op1=ALU.mult).then_inc(hn, 1)
                if tt >= 1:
                    h2_lo(tt - 1)
            ffn_lo(0, TT - 1)
            h2_lo(TT - 1)
            def gate(f, par):
                dve.wait_ge(silu_s, f + 1)
                dve.wait_ge(w_used, f * 2 + (G_OUT + 2))
                if from_(f, 2):
                    dve.wait_ge(ah_s, f - 1)
                    dve.wait_ge(al_s, f - 1)
                nc.vector.tensor_tensor(AC[:, par], ps[:, 5 + 2 * par], SG[:, par], ALU.mult).then_inc(gated_s, 1)

            def hidden_lo(f, par):
                dve.wait_ge(ah_s, f + 1)
                nc.vector.tensor_tensor(HID[:, f, 1], AC[:, par], HID[:, f, 0].bitcast(F32),
                                        ALU.subtract).then_inc(al_s, 1)

            def hidden_round(r):
                for par in range(2):
                    gate(r * 2 + par, par)
                    ffn_lo(r + 1, 2 * par)
                    hidden_lo(r * 2 + par, par)
                    ffn_lo(r + 1, 2 * par + 1)

            hidden_round(0)
            with dve.Fori(1, GATE_ROUNDS) as r:
                hidden_round(r)
            with dve.Fori(GATE_ROUNDS + 1, ROUNDS) as r:
                for n in range(4):
                    ffn_lo(r, n)
            for n in range(REST):
                ffn_lo(ROUNDS, n)
            for tt in range(TT):
                for half in range(2):
                    dve.wait_ge(y_done, 2 * tt + half + 1)
                    at = (slice(None), tt, slice(half * SEQ, (half + 1) * SEQ))
                    nc.vector.tensor_tensor(X[at], ps[:, 2 * tt + half], X[at], ALU.add).then_inc(y_add, 1)

        @block.tensor
        def _(pe):
            def product(dst, lh, ll, rh, rl, start, stop):
                nc.tensor.matmul(dst, lh, rh, start=start, stop=False, skip_group_check=True)
                nc.tensor.matmul(dst, lh, rl, start=False, stop=False, skip_group_check=True)
                return nc.tensor.matmul(dst, ll, rh, start=False, stop=stop, skip_group_check=True)

            def project(p, n):
                j, k = divmod(n, KT)
                if k == 0:
                    pe.wait_ge(w_hi, p * 3 + (j + 1))
                    pe.wait_ge(w_lo, p * 3 + (j + 1))
                    if j == 0 and from_(p, 1):
                        pe.wait_ge(v_ev, p)
                    if j == 1 and from_(p, 1):
                        pe.wait_ge(k_ev, p * 2)
                    if j == 2:
                        pe.wait_ge(q_ev, p * 2 + 2)
                if j == 0 and not from_(p, 1):
                    pe.wait_ge(hh, k + 1)
                    pe.wait_ge(hl, k + 1)
                w = slice(k * P, (k + 1) * P)
                ins = product(ps[:, j % 2], WH[:, j, w], WL[:, j, w], H1[:, k, 0], H1[:, k, 1], k == 0, k == KT - 1)
                if k == KT - 1:
                    ins.then_inc(w_used, 1)

            def mean_squares(p):
                pe.wait_ge(k_ev, p * 2 + 1)
                if from_(p, 1):
                    pe.wait_ge(vl_s, p)
                for j, SQ in enumerate((SQQ, SQK)):
                    for tt in range(TT):
                        c = 2 * (TT * j + tt)
                        ins = nc.tensor.matmul(ps[:, 7, c:c + 2], SQ[:, tt * P:(tt + 1) * P], IND, start=True, stop=True,
                                               skip_group_check=True)
                ins.then_inc(ms_s, 1)

            def spread_k(p):
                pe.wait_ge(kbc_s, p + 1)
                for tt in range(TT):
                    ins = nc.tensor.transpose(ps[:, 7, tt * P:(tt + 1) * P],
                                              KBC[:, tt].rearrange("p a e -> p (a e)"), ident[:])
                ins.then_inc(kb_s, 1)

            def turn_v(t):
                pe.wait_ge(v_scaled, t + 1)
                pe.wait_ge(kn_s, t + 1)
                for tt in range(TT):
                    ins = nc.tensor.transpose(ps[:, 7, tt * P:(tt + 1) * P], VT[:, tt * P:(tt + 1) * P], ident[:])
                ins.then_inc(v_turn, 1)

            def scores(t, qt):
                W = (qt + 1) * P
                qs = slice(qt * P, W)
                if qt == 0:
                    for parts_ready in (qh_s, ql_s, kh_s, kl_s):
                        pe.wait_ge(parts_ready, t + 1)
                if from_(t, 1) or qt >= 1:
                    pe.wait_ge(ex_s, t * 8 + 2 * qt)
                rows = (slice(0, HEAD), slice(HEAD, P))
                for n, (left, right) in enumerate(((QH, KH), (QH, KL), (QL, KH))):
                    for a in range(2):
                        ins = nc.tensor.matmul(ps[:, 2 + a, 0:W], left[rows[a], qs], right[rows[a], 0:W], start=n == 0,
                                               stop=n == 2, skip_group_check=True)
                ins.then_inc(sc_s, 1)

            def turn_p(t, qt, moba):
                for a in maps(moba):
                    n = turned(t, qt, a, moba)
                    pe.wait_ge(pn_s, n)
                    if from_(t, 1) or qt >= 1:
                        pe.wait_ge(pl_s, n - 2)
                    if qt == 1 and not moba and from_(t, MOBA_PAIRS + 1):
                        pe.wait_ge(o_add, t - MOBA_PAIRS)
                    bank = 4 + (a if moba else qt % 2)
                    for kt in range(qt + 1):
                        ins = nc.tensor.transpose(ps[:, bank, kt * P:(kt + 1) * P],
                                                  PR[qt % 2][:, a, kt * P:(kt + 1) * P], ident[:])
                    ins.then_inc(pt_s, 1)

            def heads_out(t, part, moba):
                if part == 0:
                    pe.wait_ge(pl_s, turned(t, TT - 1, 1 if moba else 0, moba))
                    pe.wait_ge(vh_s, t + 1)
                    pe.wait_ge(vl_s, t + 1)
                    if from_(t, 1):
                        pe.wait_ge(ml_s, t)
                if moba:
                    for kt in range(TT):
                        ins = product(ps[:, 6, kt * P:SEQ], VH[:, part, kt], VL[:, part, kt],
                                      PTH[:, part, kt, kt * P:SEQ], PTL[:, part, kt, kt * P:SEQ],
                                      part == 0 and kt == 0, part == 1 and kt == TT - 1)
                else:
                    for qt in ((0, 1, 2), (3,))[part]:
                        main, cross = o_columns(qt)
                        for kt in range(qt + 1):
                            qs = slice(qt * P, (qt + 1) * P)
                            nc.tensor.matmul(ps[:, 5 + qt // 2, main.start:cross.stop], PTH[:, 0, kt, qs],
                                             V[:, :, 0, kt], start=kt == 0, stop=False, skip_group_check=True)
                            ins = nc.tensor.matmul(ps[:, 5 + qt // 2, cross], PTL[:, 0, kt, qs], VH[:, 0, kt],
                                                   start=False, stop=kt == qt, skip_group_check=True)
                if part == 1:
                    ins.then_inc(pv_s, 1)

            def turn_o(t):
                pe.wait_ge(on_s, t - (MOBA_PAIRS - 1))
                for qt in range(TT):
                    ins = nc.tensor.transpose(ps[:, 6, qt * P:(qt + 1) * P], ON[:, qt], ident[:])
                ins.then_inc(o_turn, 1)

            def w_out(half, tt, k):
                cs = slice((k % 2) * SEQ, (k % 2 + 1) * SEQ)
                g = G_OUT + KT // 2 * half + k // 2
                if half == 1:
                    wh, wl = H1[:, k, 0], H1[:, k, 1]
                elif g < RING3:
                    wh, wl = WH[:, k // 2, cs], WL[:, k // 2, cs]
                else:
                    wh, wl = WO[:, 0, cs], WO[:, 1, cs]
                pe.wait_ge(w_lo, g + 1)
                pe.wait_ge(ml_s, k + 1)
                qs = slice(tt * P, (tt + 1) * P)
                ins = product(ps[:, OUT_BANKS[half][tt]], MIX[:, k, 0, qs], MIX[:, k, 1, qs], wh, wl, k == 0, k == KT - 1)
                if k == KT - 1:
                    ins.then_inc(wo_s, 1)

            pe.wait_ge(ident_in_s, 16)
            for n in range(WARM):
                nc.tensor.matmul(ps[:, 0, 0:P], ident[:], ident[:], start=True, stop=True)
            for tt in range(TT):
                pe.wait_ge(x_in[tt], 16)
                for k in range(KT):
                    ins = nc.tensor.transpose(ps[:, k, tt * P:(tt + 1) * P], X[:, tt, k * P:(k + 1) * P], ident[:])
                    if tt == TT - 1:
                        ins.then_inc(x_turned, 1)
            for n in range(12):
                project(0, n)
            pe.wait_ge(hl, KT)
            pe.wait_ge(rb_copied, 1)
            for tt in range(TT):
                ins = nc.tensor.transpose(ps[:, 7, tt * P:(tt + 1) * P], KBC[:, tt].rearrange("p a e -> p (a e)"),
                                          ident[:])
            ins.then_inc(rb_turned, 1)
            for n in range(12, 18):
                project(0, n)
            pe.wait_ge(rb_s, 1)
            mean_squares(0)
            for n in range(18, 24):
                project(0, n)

            def filler(p):
                done = [0]

                def fill(n):
                    for m in range(done[0], done[0] + n):
                        project(p, m)
                    done[0] += n
                return fill

            def out_filler():
                done = [0]

                def fill(n):
                    for m in range(done[0], done[0] + n):
                        tt, k = (m % 2, m // 2) if m < 12 else (2, m - 12) if m < 18 else (m - 18, 6)
                        if (tt, k) == (0, 0):
                            pe.wait_ge(v_ev, PAIRS)
                            pe.wait_ge(k_ev, 2 * PAIRS)
                        if (tt, k) == (2, 0):
                            pe.wait_ge(vl_s, PAIRS)
                        w_out(0, tt, k)
                    done[0] += n
                return fill

            fill = filler(1)
            spread_k(0)
            fill(4)
            scores(0, 0)
            turn_v(0)
            fill(2)
            scores(0, 1)
            fill(3)
            turn_p(0, 0, True)
            fill(1)
            scores(0, 2)
            fill(1)
            turn_p(0, 1, True)
            fill(4)
            scores(0, 3)
            fill(2)
            turn_p(0, 2, True)
            fill(5)
            turn_p(0, 3, True)
            mean_squares(1)
            fill(2)
            heads_out(0, 0, True)
            spread_k(1)
            heads_out(0, 1, True)
            with pe.Fori(1, MOBA_PAIRS) as t:
                fill = filler(t + 1)
                fill(1)
                scores(t, 0)
                fill(2)
                turn_v(t)
                fill(1)
                scores(t, 1)
                turn_p(t, 0, True)
                fill(4)
                scores(t, 2)
                fill(4)
                turn_p(t, 1, True)
                scores(t, 3)
                fill(6)
                turn_p(t, 2, True)
                mean_squares(t + 1)
                turn_p(t, 3, True)
                fill(5)
                heads_out(t, 0, True)
                spread_k(t + 1)
                fill(1)
                heads_out(t, 1, True)
            fill = filler(5)
            fill(1)
            scores(4, 0)
            fill(1)
            turn_v(4)
            fill(1)
            scores(4, 1)
            turn_p(4, 0, False)
            fill(4)
            scores(4, 2)
            fill(4)
            turn_p(4, 1, False)
            fill(1)
            scores(4, 3)
            fill(1)
            fill(5)
            turn_p(4, 2, False)
            fill(1)
            mean_squares(5)
            turn_p(4, 3, False)
            fill(5)
            heads_out(4, 0, False)
            spread_k(5)
            heads_out(4, 1, False)
            with pe.Fori(MOBA_PAIRS + 1, PAIRS - 1) as t:
                fill = filler(t + 1)
                fill(1)
                scores(t, 0)
                fill(1)
                turn_v(t)
                fill(1)
                scores(t, 1)
                turn_p(t, 0, False)
                fill(4)
                scores(t, 2)
                fill(4)
                turn_p(t, 1, False)
                fill(1)
                scores(t, 3)
                fill(1)
                turn_o(t - 1)
                fill(5)
                turn_p(t, 2, False)
                fill(1)
                mean_squares(t + 1)
                turn_p(t, 3, False)
                fill(5)
                heads_out(t, 0, False)
                spread_k(t + 1)
                heads_out(t, 1, False)
            fill = out_filler()
            turn_v(7)
            fill(1)
            scores(7, 0)
            fill(3)
            scores(7, 1)
            fill(3)
            scores(7, 2)
            fill(2)
            turn_p(7, 0, False)
            turn_p(7, 1, False)
            fill(2)
            scores(7, 3)
            turn_o(6)
            fill(5)
            turn_p(7, 2, False)
            fill(2)
            turn_p(7, 3, False)
            fill(3)
            heads_out(7, 0, False)
            heads_out(7, 1, False)
            for k in range(6):
                w_out(0, 3, k)
            for k in range(4):
                w_out(1, 0, k)
            turn_o(PAIRS - 1)
            for k in range(4, 6):
                w_out(1, 0, k)
            w_out(0, 3, 6)
            for tt in range(TT):
                w_out(0, tt, 7)

            def turn_h2(tt):
                pe.wait_ge(hn, tt + 1)
                if tt == 0:
                    pe.wait_ge(res, TT)
                else:
                    pe.wait_ge(h2l, tt)
                for k in range(KT):
                    ins = nc.tensor.transpose(ps[:, k // 4, (k % 4) * P:(k % 4 + 1) * P], HN2[:, tt, k * P:(k + 1) * P],
                                              ident[:])
                ins.then_inc(h2_turned, 1)

            for tt in range(TT):
                for k in range(6 if tt == 0 else 0, KT):
                    w_out(1, tt, k)
                if tt >= 1 and tt < 3:
                    turn_h2(tt - 1)

            def hidden(f, par, j, cols):
                pe.wait_ge(w_lo, f * 2 + (G_FFN + j + 1))
                if from_(f, 2):
                    pe.wait_ge((silu_s, gated_s)[j], f - 1)
                for k in range(KT):
                    w = slice(k * P, (k + 1) * P)
                    ins = product(ps[:, 4 + 2 * par + j, cols], WH[:, 2 * par + j, w], WL[:, 2 * par + j, w],
                                  H2[:, k, 0, cols], H2[:, k, 1, cols], k == 0, k == KT - 1)
                if cols.stop == SEQ:
                    ins.then_inc(w_used, 1)

            for n, (f, j) in enumerate(((0, 0), (0, 1), (1, 0), (1, 1))):
                pe.wait_ge(h2l, 2)
                if n < 3:
                    pe.wait_ge(res, TT + n + 1)
                hidden(f, f, j, slice(0, SEQ // 2))
                if n == 0:
                    turn_h2(2)
                if n == 2:
                    turn_h2(3)
            pe.wait_ge(h2l, TT)
            for f, j in ((0, 0), (0, 1), (1, 0), (1, 1)):
                hidden(f, f, j, slice(SEQ // 2, SEQ))
            with pe.Fori(1, GATE_ROUNDS) as r:
                for par in range(2):
                    hidden(r * 2 + par, par, 0, slice(0, SEQ))
                    hidden(r * 2 + par, par, 1, slice(0, SEQ))

            def down(f, tt, half):
                s = (G_DOWN + f) % 4
                qs, cs = slice(tt * P, (tt + 1) * P), slice(half * SEQ, (half + 1) * SEQ)
                return product(ps[:, 2 * tt + half], HID[:, f, 0, qs], HID[:, f, 1, qs], WH[:, s, cs], WL[:, s, cs],
                               f == 0, f == FT - 1)

            TAIL = 3
            for f in range(FT - TAIL):
                pe.wait_ge(w_lo, G_DOWN + f + 1)
                pe.wait_ge(al_s, f + 1)
                for tt in range(TT):
                    if f == 0 and tt == 2:
                        pe.wait_ge(gated_s, FT)
                    for half in range(2):
                        ins = down(f, tt, half)
                ins.then_inc(w_used, 1)
            pe.wait_ge(w_lo, TILES)
            pe.wait_ge(al_s, FT)
            for tt in range(TT):
                for half in range(2):
                    for f in range(FT - TAIL, FT):
                        ins = down(f, tt, half)
                    ins.then_inc(y_done, 1)


def kernel(**inputs):
    import numpy as _np
    import concourse.bacc as _bacc
    from concourse import mybir as _mybir
    from concourse.bass_utils import run_bass_kernel_spmd as _run

    a = {k: _np.ascontiguousarray(v) for k, v in inputs.items()}
    f32 = _np.float32

    def columns(w, c):
        return w[:, c:c + P].reshape(KT, P, P).transpose(1, 0, 2).reshape(P, D)

    w_in = a["w_in"][0]
    tiles = []
    for p in range(PAIRS):
        base, n = (0, p) if p < MOBA_PAIRS else (3 * MOBA_PAIRS * P, p - MOBA_PAIRS)
        for j in range(3):
            tiles.append(columns(w_in, base + (j * MOBA_PAIRS + n) * P))
    tiles += [*a["w_out"][0].reshape(KT // 2, 2, P, 2, SEQ).transpose(3, 0, 2, 1, 4).reshape(KT, P, D)]
    for f in range(FT):
        tiles.append(columns(a["w_gate"][0], f * P))
        tiles.append(columns(a["w_up"][0], f * P))
    for f in range(FT):
        tiles.append(a["w_down"][0][f * P:(f + 1) * P])

    vec = _np.zeros((P, 28), f32)
    vec[:, 0:8] = a["attn_norm"][0].reshape(KT, P).T
    for p in range(PAIRS):
        kind = "moba" if p < MOBA_PAIRS else "diff"
        vec[:, 8 + p] = _np.tile(a[kind + "_q_norm"][0], 2)
        vec[:, 16 + p] = _np.tile(a[kind + "_k_norm"][0], 2)
    vec[:, 24] = a["diff_subln"][0]
    lams = _np.concatenate([a[n][0] for n in ("lambda_q1", "lambda_k1", "lambda_q2", "lambda_k2")])

    inv = (1.0 / (f32(10000.0) ** (_np.arange(0, HEAD, 2, dtype=f32) / f32(HEAD)))).astype(f32)
    ang = _np.arange(SEQ, dtype=f32)[None, :] * inv[:, None]
    cos = _np.tile(_np.cos(ang), (4, 1)).astype(f32)
    sin = _np.tile(_np.concatenate([-_np.sin(ang), _np.sin(ang)]), (2, 1)).astype(f32)
    vec[0:HEAD, 26] = 1.0 / HEAD
    vec[HEAD:P, 27] = 1.0 / HEAD
    mask = _np.triu(_np.full((P, P), MASKED, f32), 1)

    arrays = {
        "x": a["x"].reshape(TT, P, D),
        "wt": _np.stack(tiles),
        "vec": vec,
        "gain2": _np.ascontiguousarray(_np.broadcast_to(a["ffn_norm"][0], (P, D))),
        "lams": _np.ascontiguousarray(_np.broadcast_to(lams, (P, 4 * HEAD))),
        "ident": _np.eye(P, dtype=f32),
        "mask": mask,
        "cos": cos,
        "sin": sin,
    }
    nc = _bacc.Bacc("TRN2", target_bir_lowering=False, num_devices=1)
    args = [nc.dram_tensor(n, v.shape, _mybir.dt.from_np(v.dtype), kind="ExternalInput").ap() for n, v in arrays.items()]
    out = nc.dram_tensor("out", (TT, P, D), _mybir.dt.float32, kind="ExternalOutput").ap()
    build(nc, *args, out)
    r = _run(nc, [arrays], core_ids=[0])
    return r.results[0]["out"].reshape(1, SEQ, D)
```
